# Optimizing a Trainium2 kernel written in Bass

```python
import math
import jax, jax.numpy as jnp
from jax import lax
import numpy as np

D_MODEL = 1024
BATCH = 1
SEQ = 4096
DEPTH = 1

CHUNK = 64
D_MIX = D_MODEL
SB_HEADS = 8
SB_HEAD_DIM = 64
SB_WIDTH = SB_HEADS * SB_HEAD_DIM
LRU_WIDTH = D_MIX - SB_WIDTH
LRU_BLOCKS = 8
LRU_BLOCK_W = LRU_WIDTH // LRU_BLOCKS
CONV_W = 4
RG_C = 8.0
Q_BLOCK = 128
N_GROUPS = 4
EXPERTS_PER_GROUP = 8
N_EXPERTS = N_GROUPS * EXPERTS_PER_GROUP
TOP_K_FINE = 2
D_EXPERT = 512
EPS = 1e-6
IN_COLS = 3 * SB_WIDTH + 2 * LRU_WIDTH

kernel_name = "hymba_stickbreak_rglru_hiermoe"

def _rms(x, g):
    xf = x.astype(jnp.float32)
    y = xf * lax.rsqrt(jnp.mean(xf * xf, axis=-1, keepdims=True) + EPS)
    return (y * g.astype(jnp.float32)).astype(x.dtype)

def _stick_breaking(q, k, v):
    b, h, s, d = q.shape
    nb = s // Q_BLOCK
    scale = 1.0 / math.sqrt(d)
    qb = q.reshape(b, h, nb, Q_BLOCK, d).transpose(2, 0, 1, 3, 4)
    key_pos = jnp.arange(s)

    def one_block(args):
        q_blk, blk = args
        t_pos = blk * Q_BLOCK + jnp.arange(Q_BLOCK)
        mask = key_pos[None, :] < t_pos[:, None]
        z = jnp.einsum('bhqd,bhkd->bhqk', q_blk, k).astype(jnp.float32) * scale
        log_nb_raw = jax.nn.log_sigmoid(-z)
        log_b = z + log_nb_raw
        log_nb = jnp.where(mask, log_nb_raw, 0.0)
        excl = lax.cumsum(log_nb, axis=3, reverse=True) - log_nb
        a = jnp.where(mask, jnp.exp(log_b + excl), 0.0)
        return jnp.einsum('bhqk,bhkd->bhqd', a.astype(v.dtype), v)

    out = lax.map(one_block, (qb, jnp.arange(nb)))
    return out.transpose(1, 0, 3, 2, 4).reshape(b, s, h * d)

def _causal_dwconv(x, w, bias):
    c = x.shape[-1]
    y = lax.conv_general_dilated(
        x, w.reshape(CONV_W, 1, c).astype(x.dtype), window_strides=(1,),
        padding=[(CONV_W - 1, 0)], dimension_numbers=('NWC', 'WIO', 'NWC'),
        feature_group_count=c)
    return y + bias

def _rglru(xc, w_rgate, b_rgate, w_igate, b_igate, lam):
    b, s, c = xc.shape
    xb = xc.reshape(b, s, LRU_BLOCKS, LRU_BLOCK_W)
    r = jax.nn.sigmoid(jnp.einsum('bsnc,ncd->bsnd', xb, w_rgate).reshape(b, s, c) + b_rgate)
    i = jax.nn.sigmoid(jnp.einsum('bsnc,ncd->bsnd', xb, w_igate).reshape(b, s, c) + b_igate)
    log_a = RG_C * r.astype(jnp.float32) * jax.nn.log_sigmoid(lam.astype(jnp.float32))
    a = jnp.exp(log_a)
    mult = jnp.sqrt(-jnp.expm1(2.0 * log_a))
    u = mult * (i * xc).astype(jnp.float32)

    def combine(left, right):
        a1, b1 = left
        a2, b2 = right
        return a1 * a2, a2 * b1 + b2

    _, hseq = lax.associative_scan(combine, (a, u), axis=1)
    return hseq.astype(xc.dtype)

def _hier_moe(u, w_group, b_group, w_fine, b_fine, w_e_gate, w_e_up, w_e_down):
    b, s, d = u.shape
    n = b * s
    xt = u.reshape(n, d)
    g_logits = (xt @ w_group + b_group).astype(jnp.float32)
    g_probs = jax.nn.softmax(g_logits, axis=-1)
    g_idx = jnp.argmax(g_probs, axis=-1)
    g_p = jnp.take_along_axis(g_probs, g_idx[:, None], axis=-1)
    f_logits = (xt @ w_fine + b_fine).astype(jnp.float32).reshape(n, N_GROUPS, EXPERTS_PER_GROUP)
    f_logits = jnp.take_along_axis(f_logits, g_idx[:, None, None], axis=1)[:, 0]
    f_probs = jax.nn.softmax(f_logits, axis=-1)
    top_p, top_i = lax.top_k(f_probs, TOP_K_FINE)
    top_p = top_p / jnp.sum(top_p, axis=-1, keepdims=True)
    weights = (g_p * top_p).reshape(-1)
    expert_ids = (g_idx[:, None] * EXPERTS_PER_GROUP + top_i).reshape(-1).astype(jnp.int32)
    order = jnp.argsort(expert_ids)
    tok = order // TOP_K_FINE
    xs = xt[tok]
    sizes = jnp.bincount(expert_ids, length=N_EXPERTS).astype(jnp.int32)
    hg = lax.ragged_dot(xs, w_e_gate, sizes)
    hu = lax.ragged_dot(xs, w_e_up, sizes)
    ys = lax.ragged_dot(jax.nn.silu(hg) * hu, w_e_down, sizes)
    ys = ys * weights[order][:, None].astype(ys.dtype)
    out = jnp.zeros((n, d), ys.dtype).at[tok].add(ys)
    return out.reshape(b, s, d).astype(u.dtype)

def setup_inputs(seed: int = 0) -> dict:
    key = jax.random.key(seed)
    ks = jax.random.split(key, 24)
    f32 = jnp.float32
    nrm = lambda k, shp, fan: jax.random.normal(k, shp, f32) * (fan ** -0.5)
    u_dec = jax.random.uniform(ks[10], (LRU_WIDTH,), f32, 0.9, 0.999)
    a0 = u_dec ** (1.0 / RG_C)
    lam = jnp.log(a0) - jnp.log1p(-a0)
    return {
        "x": jax.random.normal(ks[0], (BATCH, SEQ, D_MODEL), f32),
        "norm1_g": 1.0 + 0.05 * jax.random.normal(ks[1], (D_MODEL,), f32),
        "w_in": nrm(ks[2], (D_MODEL, IN_COLS), D_MODEL),
        "conv_w": nrm(ks[3], (CONV_W, LRU_WIDTH), CONV_W),
        "conv_b": 0.02 * jax.random.normal(ks[4], (LRU_WIDTH,), f32),
        "w_rgate": nrm(ks[5], (LRU_BLOCKS, LRU_BLOCK_W, LRU_BLOCK_W), LRU_BLOCK_W),
        "b_rgate": 0.02 * jax.random.normal(ks[6], (LRU_WIDTH,), f32),
        "w_igate": nrm(ks[7], (LRU_BLOCKS, LRU_BLOCK_W, LRU_BLOCK_W), LRU_BLOCK_W),
        "b_igate": 0.02 * jax.random.normal(ks[8], (LRU_WIDTH,), f32),
        "lam": lam,
        "sb_norm_g": 1.0 + 0.05 * jax.random.normal(ks[9], (SB_WIDTH,), f32),
        "lru_norm_g": 1.0 + 0.05 * jax.random.normal(ks[11], (LRU_WIDTH,), f32),
        "w_out": nrm(ks[12], (D_MIX, D_MODEL), D_MIX),
        "norm2_g": 1.0 + 0.05 * jax.random.normal(ks[13], (D_MODEL,), f32),
        "w_group": nrm(ks[14], (D_MODEL, N_GROUPS), D_MODEL),
        "b_group": 0.01 * jax.random.normal(ks[15], (N_GROUPS,), f32),
        "w_fine": nrm(ks[16], (D_MODEL, N_EXPERTS), D_MODEL),
        "b_fine": 0.01 * jax.random.normal(ks[17], (N_EXPERTS,), f32),
        "w_e_gate": nrm(ks[18], (N_EXPERTS, D_MODEL, D_EXPERT), D_MODEL),
        "w_e_up": nrm(ks[19], (N_EXPERTS, D_MODEL, D_EXPERT), D_MODEL),
        "w_e_down": nrm(ks[20], (N_EXPERTS, D_EXPERT, D_MODEL), D_EXPERT),
        "final_g": 1.0 + 0.05 * jax.random.normal(ks[21], (D_MODEL,), f32),
    }

def reference(x, norm1_g, w_in, conv_w, conv_b, w_rgate, b_rgate, w_igate, b_igate, lam,
              sb_norm_g, lru_norm_g, w_out, norm2_g, w_group, b_group, w_fine, b_fine,
              w_e_gate, w_e_up, w_e_down, final_g):
    b, s, _ = x.shape
    h = x
    for _layer in range(DEPTH):
        u = _rms(h, norm1_g)
        proj = u @ w_in
        q, k, v, x_lru, g_lru = jnp.split(
            proj, [SB_WIDTH, 2 * SB_WIDTH, 3 * SB_WIDTH, 3 * SB_WIDTH + LRU_WIDTH], axis=-1)
        to_heads = lambda t: t.reshape(b, s, SB_HEADS, SB_HEAD_DIM).transpose(0, 2, 1, 3)
        out_sb = _stick_breaking(to_heads(q), to_heads(k), to_heads(v))
        xc = _causal_dwconv(x_lru, conv_w, conv_b)
        out_lru = _rglru(xc, w_rgate, b_rgate, w_igate, b_igate, lam) * jax.nn.gelu(g_lru, approximate=True)
        mixed = jnp.concatenate([_rms(out_sb, sb_norm_g), _rms(out_lru, lru_norm_g)], axis=-1)
        h = h + mixed @ w_out
        h = h + _hier_moe(_rms(h, norm2_g), w_group, b_group, w_fine, b_fine,
                          w_e_gate, w_e_up, w_e_down)
    return _rms(h, final_g)


_drawn_inputs = setup_inputs


def setup_inputs(seed=0):
    import zlib

    import numpy as np

    out = dict(_drawn_inputs(seed))
    spreads = {}
    factors = {'b_rgate': 6.326, 'b_igate': 5.089, 'b_group': 58.7, 'b_fine': 5.428}
    for name, (base, spread) in spreads.items():
        noise = np.random.default_rng([zlib.crc32(name.encode()), seed]).standard_normal(out[name].shape)
        drawn = base * np.exp(spread * noise) if base else spread * noise
        out[name] = __import__('jax').numpy.asarray(drawn.astype(out[name].dtype))
    for name, factor in factors.items():
        out[name] = (out[name] * factor).astype(out[name].dtype)
    return out
```

```python
from contextlib import ExitStack

import numpy as np

import concourse.bass as bass
from concourse import mybir

F32 = mybir.dt.float32
F32R = mybir.dt.float32r
BF16 = mybir.dt.bfloat16
I32 = mybir.dt.int32
U32 = mybir.dt.uint32
ALU = mybir.AluOpType
ACT = mybir.ActivationFunctionType
AX = mybir.AxisListType

P = 128
D = 1024
S = 4096
DC = D // P
GT = 512
NG = S // GT
TT = GT // P
NT = S // P
HD = 64
W_SB = 512
W_LRU = 512
NP = W_SB // P
NL = W_LRU // P
CONV = 4
RG_C = 8.0
EPS = 1e-6
NGRP = 4
EPG = 8
NE = NGRP * EPG
DE = 512
FC = DE // P
TOPK = 2
MAX_TILES = S * TOPK // P + NE
WIDE = MAX_TILES + 2
MASKED = -1e30


def alloc(nc, ctx):
    held = []

    def sem(name):
        held.append(nc.alloc_semaphore(name))
        return held[-1]

    def clear():
        if held:
            nc.clear_and_free_semaphores(held)
            nc.all_engine_barrier()

    ctx.callback(clear)
    sb = lambda name, shape, dt=F32: ctx.enter_context(nc.sbuf_tensor(name, shape, dt))
    ps = lambda name, shape, dt=F32: ctx.enter_context(nc.psum_tensor(name, shape, dt))
    return sb, ps, sem


def hold(engine, k, semaphore, value):
    engine.wait_ge(semaphore, value)
    engine.sem_inc(k.passed, 1)


def f32(ap):
    return ap.bitcast(F32)


def constants(nc, k, io):
    with ExitStack() as ctx:
        sb, ps, sem = alloc(nc, ctx)
        filled, selected, loaded = sem("c_filled"), sem("c_selected"), sem("c_loaded")
        block = ctx.enter_context(nc.Block())

        @block.gpsimd
        def _(pool):
            nc.gpsimd.memset(k.ident[:], 0.0)
            nc.gpsimd.memset(k.ident_bf[:], 0.0)
            nc.gpsimd.memset(k.before[:], 1.0)
            nc.gpsimd.memset(k.ones_bf[:], 1.0)
            nc.gpsimd.memset(k.ones[:], 1.0)
            nc.gpsimd.memset(k.eps[:], EPS)
            nc.gpsimd.memset(k.mask[:], 0.0).then_inc(filled, 1)
            pool.wait_ge(filled, 1)
            for m in (k.ident, k.ident_bf):
                nc.gpsimd.affine_select(out=m[:], in_=m[:], compare_op=ALU.not_equal, fill=1.0, base=0,
                                        pattern=[[-1, P]], channel_multiplier=1)
            nc.gpsimd.affine_select(out=k.before[:], in_=k.before[:], compare_op=ALU.is_gt, fill=0.0, base=0,
                                    pattern=[[1, P]], channel_multiplier=-1)
            nc.gpsimd.affine_select(out=k.mask[:], in_=k.mask[:], compare_op=ALU.is_gt, fill=MASKED, base=0,
                                    pattern=[[P, TT], [-1, GT]], channel_multiplier=1).then_inc(selected, 1)
            pool.wait_ge(selected, 1)

        @block.sync
        def _(sp):
            with nc.allow_non_contiguous_dma(reason="parameters of a few KB, once"):
                col = lambda v: v.rearrange("(c p) -> p c", p=P)
                for dst, src in ((k.g_norm1, io.norm1_g), (k.g_mix[:, 0:NP], io.sb_norm_g),
                                 (k.g_mix[:, NP:2 * NP], io.lru_norm_g), (k.conv_b, io.conv_b),
                                 (k.b_r, io.b_rgate), (k.b_i, io.b_igate), (k.lam, io.lam)):
                    sp.dma_start(dst[:], col(src)).then_inc(loaded, 16)
                sp.dma_start(k.conv_w[:], io.conv_w.rearrange("t (c p) -> p t c", p=P)).then_inc(loaded, 16)
            for dst, src in ((k.b_router[:, 0:NGRP], io.b_group), (k.b_router[:, NGRP:], io.b_fine)):
                sp.dma_start(dst, src.unsqueeze(0).partition_broadcast(P)).then_inc(loaded, 16)
            sp.wait_ge(loaded, 10 * 16)

        @block.vector
        def _(dve):
            dve.wait_ge(selected, 1)
            nc.vector.tensor_copy(k.ident_r[:], k.ident[:]).then_inc(filled, 1)
            dve.wait_ge(filled, 2)


class NormedGroups:

    def __init__(self, nc, k, io, sb, ps, sem, tag):
        self.nc, self.k, self.io = nc, k, io
        self.x = sb(tag + "x", [P, TT, D])
        self.junk = sb(tag + "junk", [P, D])
        self.sumsq = sb(tag + "sumsq", [P, TT])
        self.rms = sb(tag + "rms", [P, TT])
        self.rinv = sb(tag + "rinv", [P, TT])
        self.hi = sb(tag + "u_hi", [P, DC, GT], F32R)
        self.lo = sb(tag + "u_lo", [P, DC, GT], F32R)
        self.tr = [ps(f"{tag}tr{i}", [P, GT]) for i in range(2)]
        self.x_loaded = [sem(f"{tag}x_loaded{t}") for t in range(TT)]
        self.squared = sem(tag + "squared")
        self.rms_ready = sem(tag + "rms_ready")
        self.rinv_ready = sem(tag + "rinv_ready")
        self.x_scaled = sem(tag + "x_scaled")
        self.transposed = sem(tag + "transposed")
        self.hi_ready = sem(tag + "hi_ready")
        self.lo_ready = sem(tag + "lo_ready")

    def load(self, sp, G):
        for t in range(TT):
            sp.dma_start(self.x[:, t, :], self.io.x[bass.ds(G * GT + t * P, P), :]).then_inc(self.x_loaded[t], 16)

    def load_after(self, sp, G):
        hold(sp, self.k, self.transposed, G * DC + DC)
        self.load(sp, G + 1)

    def norm(self, act, G):
        nc = self.nc
        for t in range(TT):
            act.wait_ge(self.x_loaded[t], G * 16 + 16)
            if t > 0:
                act.wait_ge(self.squared, G * TT + t)
            nc.scalar.activation(self.junk[:], self.x[:, t, :], ACT.Square,
                                 accum_out=self.sumsq[:, t:t + 1]).then_inc(self.squared, 1)
        act.wait_ge(self.squared, G * TT + TT)
        nc.scalar.activation(self.rms[:], self.sumsq[:], ACT.Sqrt, scale=1.0 / D,
                             bias=self.k.eps[:]).then_inc(self.rms_ready, 1)

    def scale(self, dve, G):
        nc = self.nc
        dve.wait_ge(self.rms_ready, G + 1)
        nc.vector.reciprocal(self.rinv[:], self.rms[:]).then_inc(self.rinv_ready, 1)
        dve.wait_ge(self.rinv_ready, G + 1)
        for t in range(TT):
            nc.vector.tensor_scalar(self.x[:, t, :], self.x[:, t, :], self.rinv[:, t:t + 1], None,
                                    ALU.mult).then_inc(self.x_scaled, 1)

    def transpose(self, pe, G, c):
        nc = self.nc
        if c == 0:
            pe.wait_ge(self.x_scaled, G * TT + TT)
        pe.wait_ge(self.lo_ready, G * DC + c + 1)
        for t in range(TT):
            last = nc.tensor.transpose(self.tr[c % 2][:, t * P:(t + 1) * P], self.x[:, t, c * P:(c + 1) * P],
                                       self.k.ident[:])
        last.then_inc(self.transposed, 1)

    def high(self, act, G):
        nc = self.nc
        for c in range(DC):
            act.wait_ge(self.transposed, G * DC + c + 1)
            nc.scalar.activation(self.hi[:, c, :], self.tr[c % 2][:], ACT.Copy,
                                 scale=self.k.g_norm1[:, c:c + 1]).then_inc(self.hi_ready, 1)

    def low(self, dve, G):
        nc = self.nc
        for c in range(DC):
            dve.wait_ge(self.hi_ready, G * DC + c + 1)
            nc.vector.scalar_tensor_tensor(self.lo[:, c, :], self.tr[c % 2][:], self.k.g_norm1[:, c:c + 1],
                                           f32(self.hi[:, c, :]), ALU.mult, ALU.subtract).then_inc(self.lo_ready, 1)

    def product(self, pe, G, bank, w_hi, w_lo, col, chunks):
        nc = self.nc
        for c in chunks:
            pe.wait_ge(self.lo_ready, G * DC + c + 3)
            for n, (w, u) in enumerate(((w_hi, self.hi), (w_hi, self.lo), (w_lo, self.hi))):
                last = nc.tensor.matmul(bank[:], w[:, c, col:col + P], u[:, c, :],
                                        start=(c == 0 and n == 0), stop=(c == DC - 1 and n == 2))
        return last

    def leading_product(self, pe, G, bank, w_hi, w_lo):
        self.transpose(pe, G, 0)
        self.transpose(pe, G, 1)
        for c in range(DC):
            last = self.product(pe, G, bank, w_hi, w_lo, 0, [c])
            if c + 2 < DC:
                self.transpose(pe, G, c + 2)
        return last


def split_weights(nc, src, cols, w_hi, w_lo, sb, sem, tag, gain=None):
    with ExitStack() as ctx:
        sb, ps, sem = alloc(nc, ctx)
        raw = sb(tag + "w_raw", [P, 2, cols])
        arrived = [sem(f"{tag}arrived{i}") for i in range(2)]
        high, low = sem(tag + "high"), sem(tag + "low")
        block = ctx.enter_context(nc.Block())

        @block.sync
        def _(sp):
            for c in range(DC):
                if c >= 2:
                    sp.wait_ge(low, c - 1)
                sp.dma_start(raw[:, c % 2, :], src[c * P:(c + 1) * P, :]).then_inc(arrived[c % 2], 16)

        @block.scalar
        def _(act):
            for c in range(DC):
                act.wait_ge(arrived[c % 2], 16 * (c // 2 + 1))
                nc.scalar.activation(w_hi[:, c, :], raw[:, c % 2, :], ACT.Copy,
                                     scale=1.0 if gain is None else gain[:, c:c + 1]).then_inc(high, 1)

        @block.vector
        def _(dve):
            for c in range(DC):
                dve.wait_ge(high, c + 1)
                nc.vector.scalar_tensor_tensor(w_lo[:, c, :], raw[:, c % 2, :],
                                               1.0 if gain is None else gain[:, c:c + 1], f32(w_hi[:, c, :]),
                                               ALU.mult, ALU.subtract).then_inc(low, 1)


def qkv(nc, k, io):
    with ExitStack() as outer:
        sb, ps, sem = alloc(nc, outer)
        cols = 3 * W_SB
        w_hi = sb("qkv_w_hi", [P, DC, cols], F32R)
        w_lo = sb("qkv_w_lo", [P, DC, cols], F32R)
        split_weights(nc, io.w_in[:, 0:cols], cols, w_hi, w_lo, sb, sem, "qkv_")
        with ExitStack() as ctx:
            sb, ps, sem = alloc(nc, ctx)
            ug = NormedGroups(nc, k, io, sb, ps, sem, "qkv_")
            out = [ps(f"qkv_out{i}", [P, GT]) for i in range(4)]
            dv_tr = [ps(f"qkv_dv_tr{i}", [P, GT]) for i in range(2)]
            st_hi = [sb(f"qkv_st_hi{i}", [P, GT], F32R) for i in range(4)]
            st_lo = [sb(f"qkv_st_lo{i}", [P, GT], F32R) for i in range(4)]
            v = sb("qkv_v", [P, NP, GT + 1])
            dv = sb("qkv_dv", [P, NP, GT])
            st_dv = [sb(f"qkv_st_dv{i}", [P, GT]) for i in range(2)]
            v_done = sem("qkv_v_done")
            v_copied = sem("qkv_v_copied")
            v_zeroed = sem("qkv_v_zeroed")
            dv_ready = sem("qkv_dv_ready")
            v_carried = sem("qkv_v_carried")
            dv_transposed = sem("qkv_dv_transposed")
            dv_staged = sem("qkv_dv_staged")
            dv_stored = [sem(f"qkv_dv_stored{i}") for i in range(2)]
            qk_done = sem("qkv_qk_done")
            qk_high = sem("qkv_qk_high")
            qk_low = sem("qkv_qk_low")
            qk_stored = [sem(f"qkv_qk_stored{i}") for i in range(4)]
            zeros = sb("qkv_zeros", [P, D])
            cleared = sem("qkv_cleared")
            block = ctx.enter_context(nc.Block())

            @block.gpsimd
            def _(pool):
                nc.gpsimd.memset(zeros[:], 0.0).then_inc(cleared, 1)
                pool.wait_ge(cleared, 1)
                with pool.Fori(S * TOPK // P, MAX_TILES) as T:
                    pool.dma_start(io.ys[bass.ds(T * P, P), :], zeros[:]).then_inc(k.spare_filled, 16)
                pool.wait_ge(k.spare_filled, 16 * (MAX_TILES - S * TOPK // P))

            @block.tensor
            def _(pe):
                with pe.Fori(0, NG) as G:
                    for j in range(NP):
                        pe.wait_ge(qk_low, G * 8 + j + 1)
                        if j == 0:
                            last = ug.leading_product(pe, G, out[0], w_hi[:, :, 2 * W_SB:], w_lo[:, :, 2 * W_SB:])
                        else:
                            last = ug.product(pe, G, out[j], w_hi, w_lo, 2 * W_SB + j * P, range(DC))
                        last.then_inc(v_done, 1)
                    for j in range(NP):
                        pe.wait_ge(v_copied, G * NP + j + 1)
                        ug.product(pe, G, out[j], w_hi, w_lo, j * P, range(DC)).then_inc(qk_done, 1)
                    for j in range(NP):
                        pe.wait_ge(dv_ready, G * NP + j + 1)
                        pe.wait_ge(dv_staged, G * NP + j + 1)
                        for b in range(TT):
                            last = nc.tensor.transpose(dv_tr[j % 2][:, b * P:(b + 1) * P],
                                                       dv[:, j, b * P:(b + 1) * P], k.ident[:])
                        last.then_inc(dv_transposed, 1)
                    for j in range(NP):
                        pe.wait_ge(qk_low, G * 8 + j + 5)
                        ug.product(pe, G, out[j], w_hi, w_lo, W_SB + j * P, range(DC)).then_inc(qk_done, 1)

            def split_high(act, G, m):
                act.wait_ge(qk_done, G * 8 + m + 1)
                act.wait_ge(qk_stored[m % 4], G * 64 + (m // 4) * 32 + 32)
                nc.scalar.activation(st_hi[m % 4][:], out[m % 4][:], ACT.Copy).then_inc(qk_high, 1)

            def act_group(act, G, last):
                ug.high(act, G)
                for j in range(NP):
                    act.wait_ge(v_done, G * NP + j + 1)
                    act.wait_ge(v_carried, G * NP + j + 1)
                    nc.scalar.activation(v[:, j, 1:GT + 1], out[j][:], ACT.Copy).then_inc(v_copied, 1)
                    if j == 1 and not last:
                        ug.norm(act, G + 1)
                for m in range(4):
                    split_high(act, G, m)
                for j in range(NP):
                    act.wait_ge(dv_transposed, G * NP + j + NP + 1)
                    act.wait_ge(dv_stored[j % 2], G * 32 + (j // 2) * 16 + 16)
                    nc.scalar.activation(st_dv[j % 2][:], dv_tr[j % 2][:], ACT.Copy).then_inc(dv_staged, 1)
                for m in range(4, 8):
                    split_high(act, G, m)

            @block.scalar
            def _(act):
                ug.norm(act, 0)
                with act.Fori(0, NG - 1) as G:
                    act_group(act, G, False)
                act_group(act, NG - 1, True)

            def split_low(dve, G, m):
                dve.wait_ge(qk_high, G * 8 + m + 1)
                nc.vector.tensor_tensor(st_lo[m % 4][:], out[m % 4][:], f32(st_hi[m % 4][:]),
                                        ALU.subtract).then_inc(qk_low, 1)

            def dve_group(dve, G, last):
                ug.low(dve, G)
                for j in range(NP):
                    dve.wait_ge(v_copied, G * NP + j + 1)
                    dve.wait_ge(dv_transposed, G * NP + j + 1)
                    nc.vector.tensor_tensor(dv[:, j, :], v[:, j, 0:GT], v[:, j, 1:GT + 1],
                                            ALU.subtract).then_inc(dv_ready, 1)
                    nc.vector.tensor_copy(k.v_last[:, bass.ds(G + j * NG, 1)], v[:, j, GT:GT + 1])
                    dve.wait_ge(dv_ready, G * NP + j + 1)
                    nc.vector.tensor_copy(v[:, j, 0:1], v[:, j, GT:GT + 1]).then_inc(v_carried, 1)
                    if j == 1 and not last:
                        ug.scale(dve, G + 1)
                for m in range(8):
                    split_low(dve, G, m)

            @block.vector
            def _(dve):
                nc.vector.memset(v[:], 0.0).then_inc(v_zeroed, 1)
                dve.wait_ge(v_zeroed, 1)
                dve.sem_inc(v_carried, NP)
                dve.sem_inc(ug.lo_ready, 2)
                dve.sem_inc(qk_low, 4)
                dve.sem_inc(dv_transposed, NP)
                dve.sem_inc(dv_staged, 2)
                ug.scale(dve, 0)
                with dve.Fori(0, NG - 1) as G:
                    dve_group(dve, G, False)
                dve_group(dve, NG - 1, True)

            def store_qk(sp, G, m):
                dst_hi, dst_lo = (io.q_hi, io.q_lo) if m < 4 else (io.k_hi, io.k_lo)
                hold(sp, k, qk_low, G * 8 + m + 5)
                rows = slice((m % 4) * P, (m % 4 + 1) * P)
                sp.dma_start(dst_hi[rows, bass.ds(G * GT, GT)], f32(st_hi[m % 4][:])).then_inc(qk_stored[m % 4], 16)
                sp.dma_start(dst_lo[rows, bass.ds(G * GT, GT)], f32(st_lo[m % 4][:])).then_inc(qk_stored[m % 4], 16)

            def sp_group(sp, G, last):
                if not last:
                    ug.load_after(sp, G)
                for m in range(4):
                    store_qk(sp, G, m)
                for j in range(NP):
                    hold(sp, k, dv_staged, G * NP + j + 3)
                    dst = io.dv[bass.ds(G * GT, GT), j * P:(j + 1) * P].rearrange("(b p) c -> p b c", p=P)
                    sp.dma_start(dst, st_dv[j % 2][:].rearrange("p (b c) -> p b c", b=TT)).then_inc(dv_stored[j % 2], 16)
                for m in range(4, 8):
                    store_qk(sp, G, m)

            @block.sync
            def _(sp):
                for s in qk_stored:
                    sp.sem_inc(s, 32)
                for s in dv_stored:
                    sp.sem_inc(s, 16)
                ug.load(sp, 0)
                with sp.Fori(0, NG - 1) as G:
                    sp_group(sp, G, False)
                sp_group(sp, NG - 1, True)
                for s in qk_stored:
                    sp.wait_ge(s, 32 * (2 * NG + 1))
                for s in dv_stored:
                    sp.wait_ge(s, 16 * (2 * NG + 1))


def lru(nc, k, io):
    with ExitStack() as outer:
        sb, ps, sem = alloc(nc, outer)
        cols = 2 * W_LRU
        w_hi = sb("lru_w_hi", [P, DC, cols], F32R)
        w_lo = sb("lru_w_lo", [P, DC, cols], F32R)
        gates = sb("lru_gates", [P, 2, NL, P])
        slope = sb("lru_slope", [P, NL])
        neg_slope = sb("lru_neg_slope", [P, NL])
        split_weights(nc, io.w_in[:, 3 * W_SB:], cols, w_hi, w_lo, sb, sem, "lru_")

        with ExitStack() as ctx:
            sb, ps, sem = alloc(nc, ctx)
            e, w, w2, acc, relu = (sb("lru_lam_" + n, [P, NL]) for n in ("e", "w", "w2", "acc", "relu"))
            cleared, gates_loaded = sem("lru_cleared"), sem("lru_gates_loaded")
            exp_ready, step = sem("lru_exp_ready"), sem("lru_step")
            block = ctx.enter_context(nc.Block())

            @block.gpsimd
            def _(pool):
                nc.gpsimd.memset(gates[:], 0.0).then_inc(cleared, 1)

            @block.sync
            def _(sp):
                sp.wait_ge(cleared, 1)
                for n, src in enumerate((io.w_rgate, io.w_igate)):
                    for half in range(2):
                        lanes = slice(64 * half, 64 * half + 64)
                        sp.dma_start(gates[lanes, n, :, 64 * half:64 * half + 64],
                                     src.rearrange("(j half) c d -> half c j d", half=2)[half]).then_inc(gates_loaded, 16)
                sp.wait_ge(gates_loaded, 64)

            @block.scalar
            def _(act):
                act.wait_ge(step, 2)
                nc.scalar.activation(e[:], relu[:], ACT.Exp, scale=-1.0).then_inc(exp_ready, 1)

            @block.vector
            def _(dve):
                count = [0]

                def link(instruction):
                    count[0] += 1
                    instruction.then_inc(step, 1)
                    dve.wait_ge(step, count[0])

                link(nc.vector.tensor_scalar(w[:], k.lam[:], -1.0, None, ALU.mult))
                link(nc.vector.tensor_tensor(relu[:], k.lam[:], w[:], ALU.max))
                dve.wait_ge(exp_ready, 1)
                link(nc.vector.tensor_scalar(w[:], e[:], 2.0, None, ALU.add))
                link(nc.vector.reciprocal(w2[:], w[:]))
                link(nc.vector.tensor_tensor(w[:], w2[:], e[:], ALU.mult))
                link(nc.vector.tensor_tensor(w2[:], w[:], w[:], ALU.mult))
                terms = 10
                link(nc.vector.memset(acc[:], 1.0 / (2 * terms + 1)))
                for n in range(terms - 1, -1, -1):
                    link(nc.vector.tensor_tensor(e[:], acc[:], w2[:], ALU.mult))
                    link(nc.vector.tensor_scalar(acc[:], e[:], 1.0 / (2 * n + 1), None, ALU.add))
                link(nc.vector.tensor_tensor(e[:], acc[:], w[:], ALU.mult))
                link(nc.vector.tensor_scalar(w[:], e[:], -2.0 * RG_C, None, ALU.mult))
                link(nc.vector.tensor_scalar(relu[:], k.lam[:], 0.0, RG_C, ALU.min, ALU.mult))
                link(nc.vector.tensor_tensor(slope[:], relu[:], w[:], ALU.add))
                link(nc.vector.tensor_scalar(neg_slope[:], slope[:], -1.0, None, ALU.mult))

        with ExitStack() as ctx:
            sb, ps, sem = alloc(nc, ctx)
            ug = NormedGroups(nc, k, io, sb, ps, sem, "lru_")
            out = [ps(f"lru_out{i}", [P, GT]) for i in range(4)]
            gate_out = [ps(f"lru_gate_out{i}", [P, GT]) for i in range(2)]
            H = CONV - 1
            xl = sb("lru_xl", [P, NL, GT + H])
            xc = sb("lru_xc", [P, 2, NL, GT])
            gelu = sb("lru_gelu", [P, NL, GT])
            r = sb("lru_r", [P, NL, GT])
            ig = sb("lru_ig", [P, NL, GT])
            a = sb("lru_a", [P, NL, GT])
            th = sb("lru_th", [P, NL, GT])
            sq = sb("lru_sq", [P, NL, GT])
            h = r
            state = sb("lru_state", [P, NL])
            x_done = sem("lru_x_done")
            x_copied = sem("lru_x_copied")
            x_carried = sem("lru_x_carried")
            g_done = sem("lru_g_done")
            g_ready = sem("lru_g_ready")
            conv_step = sem("lru_conv_step")
            xc_ready = sem("lru_xc_ready")
            gate_done = sem("lru_gate_done")
            r_ready = sem("lru_r_ready")
            i_ready = sem("lru_i_ready")
            ix_ready = sem("lru_ix_ready")
            a_ready = sem("lru_a_ready")
            th_ready = sem("lru_th_ready")
            sq_ready = sem("lru_sq_ready")
            m2_ready = sem("lru_m2_ready")
            m_ready = sem("lru_m_ready")
            in_ready = sem("lru_in_ready")
            h_ready = sem("lru_h_ready")
            state_ready = sem("lru_state_ready")
            out_ready = sem("lru_out_ready")
            stored = [sem(f"lru_stored{j}") for j in range(NL)]
            zeroed = sem("lru_zeroed")
            block = ctx.enter_context(nc.Block())

            def sp_group(sp, G, last):
                if not last:
                    ug.load_after(sp, G)

            def sp_stores(sp, G):
                for j in range(NL):
                    hold(sp, k, out_ready, G * NL + j + NL + 1)
                    sp.dma_start(io.mix_t[W_SB + j * P:W_SB + (j + 1) * P, bass.ds(G * GT, GT)],
                                 sq[:, j, :]).then_inc(stored[j], 16)

            @block.sync
            def _(sp):
                for s in stored:
                    sp.sem_inc(s, 16)
                ug.load(sp, 0)
                sp_group(sp, 0, False)
                with sp.Fori(1, NG - 1) as G:
                    sp_group(sp, G, False)
                    sp_stores(sp, G - 1)
                sp_stores(sp, NG - 2)
                sp_stores(sp, NG - 1)
                for s in stored:
                    sp.wait_ge(s, 16 * (NG + 1))

            @block.tensor
            def _(pe):
                with pe.Fori(0, NG) as G:
                    for j in range(NL):
                        pe.wait_ge(g_ready, G * NL + j + 1)
                        if j == 0:
                            last = ug.leading_product(pe, G, out[0], w_hi, w_lo)
                        else:
                            last = ug.product(pe, G, out[j], w_hi, w_lo, j * P, range(DC))
                        last.then_inc(x_done, 1)
                    for j in range(NL):
                        pe.wait_ge(x_copied, G * NL + j + 1)
                        ug.product(pe, G, out[j], w_hi, w_lo, W_LRU + j * P, range(DC)).then_inc(g_done, 1)
                    for j in range(NL):
                        pe.wait_ge(xc_ready, G * NL + j + 1)
                        for n, free in enumerate((r_ready, i_ready)):
                            pe.wait_ge(free, G * NL + j + 1)
                            nc.tensor.matmul(gate_out[n][:], gates[:, n, j, :], xc[:, 1, j, :],
                                             start=True, stop=True).then_inc(gate_done, 1)

            def act_middle(act, G, last):
                for j in range(NL):
                    act.wait_ge(x_done, G * NL + j + 1)
                    act.wait_ge(x_carried, G * NL + j + 1)
                    nc.scalar.activation(xl[:, j, H:], out[j][:], ACT.Copy).then_inc(x_copied, 1)
                if not last:
                    ug.norm(act, G + 1)
                for j in range(NL):
                    act.wait_ge(g_done, G * NL + j + 1)
                    act.wait_ge(out_ready, G * NL + j + 1)
                    nc.scalar.activation(gelu[:, j, :], out[j][:], ACT.Gelu_apprx_tanh).then_inc(g_ready, 1)
                for j in range(NL):
                    act.wait_ge(gate_done, G * 2 * NL + 2 * j + 1)
                    nc.scalar.activation(r[:, j, :], gate_out[0][:], ACT.Sigmoid,
                                         bias=k.b_r[:, j:j + 1]).then_inc(r_ready, 1)
                    act.wait_ge(gate_done, G * 2 * NL + 2 * j + 2)
                    act.wait_ge(in_ready, G * NL + j + 1)
                    nc.scalar.activation(ig[:, j, :], gate_out[1][:], ACT.Sigmoid,
                                         bias=k.b_i[:, j:j + 1]).then_inc(i_ready, 1)

            def act_tail(act, G):
                for j in range(NL):
                    act.wait_ge(r_ready, G * NL + j + 2)
                    act.wait_ge(h_ready, G * NL + j + 1)
                    nc.scalar.activation(a[:, j, :], r[:, j, :], ACT.Exp, scale=slope[:, j:j + 1]).then_inc(a_ready, 1)
                    act.wait_ge(in_ready, G * NL + j + 1)
                    nc.scalar.activation(th[:, j, :], r[:, j, :], ACT.Tanh,
                                         scale=neg_slope[:, j:j + 1]).then_inc(th_ready, 1)
                for j in range(NL):
                    act.wait_ge(m2_ready, G * NL + j + 1)
                    nc.scalar.activation(th[:, j, :], th[:, j, :], ACT.Sqrt).then_inc(m_ready, 1)

            @block.scalar
            def _(act):
                ug.norm(act, 0)
                ug.high(act, 0)
                act_middle(act, 0, False)
                with act.Fori(1, NG - 1) as G:
                    ug.high(act, G)
                    act_tail(act, G - 1)
                    act_middle(act, G, False)
                ug.high(act, NG - 1)
                act_tail(act, NG - 2)
                act_middle(act, NG - 1, True)
                act_tail(act, NG - 1)

            def dve_middle(dve, G, last):
                for j in range(NL):
                    dve.wait_ge(x_copied, G * NL + j + 1)
                    dve.wait_ge(ix_ready, G * NL + j + 1)
                    nc.vector.tensor_scalar(xc[:, 0, j, :], xl[:, j, H:H + GT], k.conv_w[:, H, j:j + 1],
                                            k.conv_b[:, j:j + 1], ALU.mult, ALU.add).then_inc(conv_step, 1)
                    for n, tap in enumerate(range(H - 1, -1, -1)):
                        dve.wait_ge(conv_step, (G * NL + j) * H + n + 1)
                        last_step = nc.vector.scalar_tensor_tensor(
                            xc[:, (n + 1) % 2, j, :], xl[:, j, tap:tap + GT], k.conv_w[:, tap, j:j + 1],
                            xc[:, n % 2, j, :], ALU.mult, ALU.add)
                        last_step.then_inc(conv_step if tap else xc_ready, 1)
                    dve.wait_ge(xc_ready, G * NL + j + 1)
                    nc.vector.tensor_copy(xl[:, j, 0:H], xl[:, j, GT:GT + H]).then_inc(x_carried, 1)
                if not last:
                    ug.scale(dve, G + 1)
                for j in range(NL):
                    dve.wait_ge(i_ready, G * NL + j + 2)
                    nc.vector.tensor_tensor(ig[:, j, :], ig[:, j, :], xc[:, 1, j, :], ALU.mult).then_inc(ix_ready, 1)

            def dve_tail(dve, G):
                for j in range(NL):
                    dve.wait_ge(th_ready, G * NL + j + NL + 1)
                    dve.wait_ge(sq_ready, G * NL + j + 1)
                    nc.vector.scalar_tensor_tensor(th[:, j, :], sq[:, j, :], 1.0, th[:, j, :], ALU.add,
                                                   ALU.mult).then_inc(m2_ready, 1)
                for j in range(NL):
                    dve.wait_ge(in_ready, G * NL + j + NL + 1)
                    dve.wait_ge(state_ready, G * NL + j + 1)
                    dve.wait_ge(out_ready, G * NL + j + 1)
                    nc.vector.tensor_tensor_scan(h[:, j, :], a[:, j, :], sq[:, j, :], state[:, j:j + 1],
                                                 ALU.mult, ALU.add).then_inc(h_ready, 1)
                for j in range(NL):
                    dve.wait_ge(h_ready, G * NL + j + NL + 1)
                    nc.vector.tensor_copy(state[:, j:j + 1], h[:, j, GT - 1:GT]).then_inc(state_ready, 1)
                    nc.vector.tensor_tensor(sq[:, j, :], h[:, j, :], gelu[:, j, :], ALU.mult).then_inc(out_ready, 1)

            @block.vector
            def _(dve):
                nc.vector.memset(xl[:], 0.0).then_inc(zeroed, 1)
                nc.vector.memset(state[:], 0.0).then_inc(zeroed, 1)
                dve.wait_ge(zeroed, 2)
                dve.sem_inc(x_carried, NL)
                dve.sem_inc(state_ready, NL)
                dve.sem_inc(ug.lo_ready, 2)
                dve.sem_inc(g_ready, NL)
                dve.sem_inc(out_ready, NL)
                dve.sem_inc(r_ready, 1)
                dve.sem_inc(i_ready, 1)
                dve.sem_inc(th_ready, NL)
                dve.sem_inc(h_ready, NL)
                dve.sem_inc(in_ready, NL)
                dve.sem_inc(ix_ready, NL)
                ug.scale(dve, 0)
                ug.low(dve, 0)
                dve_middle(dve, 0, False)
                with dve.Fori(1, NG - 1) as G:
                    ug.low(dve, G)
                    dve_tail(dve, G - 1)
                    dve_middle(dve, G, False)
                ug.low(dve, NG - 1)
                dve_tail(dve, NG - 2)
                dve_middle(dve, NG - 1, True)
                dve_tail(dve, NG - 1)

            @block.gpsimd
            def _(pool):
                with pool.Fori(0, NG) as G:
                    for j in range(NL):
                        pool.wait_ge(a_ready, G * NL + j + 1)
                        pool.wait_ge(stored[j], G * 16 + 16)
                        nc.gpsimd.tensor_tensor(sq[:, j, :], a[:, j, :], a[:, j, :], ALU.mult).then_inc(sq_ready, 1)
                    for j in range(NL):
                        pool.wait_ge(m_ready, G * NL + j + 1)
                        pool.wait_ge(ix_ready, G * NL + j + NL + 1)
                        nc.gpsimd.tensor_tensor(sq[:, j, :], th[:, j, :], ig[:, j, :], ALU.mult).then_inc(in_ready, 1)


def attention(nc, k, io):
    units = [(G, c) for G in range(NG) for c in range(G, -1, -1)]
    U = len(units)
    K = 4 * U
    LT = 6
    LA = LT + 1
    scale = HD ** -0.5
    with ExitStack() as ctx:
        sb, ps, sem = alloc(nc, ctx)
        q = sb("att_q", [P, 2, S], F32R)
        k_hi = sb("att_k_hi", [P, 2, S], F32R)
        k_lo = sb("att_k_lo", [P, 2, S], F32R)
        dv = sb("att_dv", [P, NT, P])
        stay = sb("att_stay", [P, 4, 2 * GT])
        R = sb("att_R", [P, 3, 2, TT, GT])
        RT = sb("att_RT", [P, 2, 4, GT])
        stage = sb("att_stage", [P, 2, GT])
        z = [ps(f"att_z{i}", [P, 2 * GT]) for i in range(2)]
        rt = [ps(f"att_rt{i}", [P, GT]) for i in range(2)]
        out = [ps(f"att_out{i}", [P, GT]) for i in range(2)]
        chunk_loaded = [sem(f"att_chunk_loaded{g}") for g in range(NG)]
        z_done = sem("att_z_done")
        stay_ready = sem("att_stay_ready")
        scanned = sem("att_scanned")
        rt_done = [sem(f"att_rt_done{h}") for h in range(2)]
        rt_copied = [sem(f"att_rt_copied{h}") for h in range(2)]
        av_done = sem("att_av_done")
        out_copied = sem("att_out_copied")
        stored = [sem(f"att_stored{i}") for i in range(2)]
        LOADS = 7
        block = ctx.enter_context(nc.Block())

        def load_rows(sp, hp, g, dst, src_low, src_high):
            cols = slice(g * GT, (g + 1) * GT)
            for lanes, src in ((slice(0, HD), src_low), (slice(HD, P), src_high)):
                sp.dma_start(f32(dst[lanes, :, cols]), src[bass.ds(hp * P, P), cols].rearrange("(h p) s -> p h s", h=2)
                             ).then_inc(chunk_loaded[g], 16)

        def load_queries(sp, hp, g):
            load_rows(sp, hp, g, q, io.q_hi, io.q_lo)

        def load_keys(sp, hp, g):
            load_rows(sp, hp, g, k_hi, io.k_hi, io.k_hi)
            load_rows(sp, hp, g, k_lo, io.k_lo, io.k_lo)
            cols = slice(g * GT, (g + 1) * GT)
            sp.dma_start(dv[:, g * TT:(g + 1) * TT, :],
                         io.dv[cols, bass.ds(hp * P, P)].rearrange("(t p) c -> p t c", p=P)).then_inc(chunk_loaded[g], 16)

        @block.sync
        def _(sp):
            for g in range(NG):
                load_queries(sp, 0, g)
                load_keys(sp, 0, g)
            with sp.Fori(1, NP) as hp:
                for g in range(NG - 1, -1, -1):
                    hold(sp, k, av_done, 4 + (hp - 1) * K + 4 * (units.index((NG - 1, g)) + 1))
                    load_keys(sp, hp, g)
                    if g < NG - 1:
                        load_queries(sp, hp, g)
                load_queries(sp, hp, NG - 1)

        def scores(pe, hp, step):
            n, s = divmod(step, 4)
            G, c = units[n]
            h = s // 2
            if s == 0 and c == G:
                pe.wait_ge(chunk_loaded[G], hp * 16 * LOADS + 16 * LOADS)
            pe.wait_ge(stay_ready, hp * K + step + 1)
            for i in range(2):
                qt = 2 * (s % 2) + i
                bank = z[step % 2][:, i * GT:(i + 1) * GT]
                q_tile = q[:, h, G * GT + qt * P:G * GT + (qt + 1) * P]
                keys = slice(c * GT, (c + 1) * GT)
                nc.tensor.matmul(bank, q_tile, k_hi[:, h, keys], start=True, stop=False)
                last = nc.tensor.matmul(bank, q_tile, k_lo[:, h, keys], start=False, stop=(c != G))
                if c == G:
                    last = nc.tensor.matmul(bank, k.ident_bf[:], k.mask[:, qt, :], start=False, stop=True)
            last.then_inc(z_done, 1)

        def transposes(pe, hp, step):
            n, s = divmod(step, 4)
            for h in range(2):
                pe.wait_ge(scanned, 8 + hp * 8 * U + 8 * n + 4 * h + 4)
                pe.wait_ge(rt_copied[h], hp * K + step + 1)
                for qt in range(TT):
                    last = nc.tensor.transpose(rt[h][:, qt * P:(qt + 1) * P], R[:, n % 3, h, qt, s * P:(s + 1) * P],
                                               k.ident[:])
                last.then_inc(rt_done[h], 1)

        def values(pe, hp, step):
            n, s = divmod(step, 4)
            G, c = units[n]
            if c == G and s == 0:
                pe.wait_ge(out_copied, hp * NG + G + 1)
            for h in range(2):
                pe.wait_ge(rt_copied[h], hp * K + step + 2)
            for h in range(2):
                last = nc.tensor.matmul(out[G % 2][h * HD:(h + 1) * HD, :], dv[:, c * TT + s, h * HD:(h + 1) * HD],
                                        RT[:, h, s, :], start=(c == G and s == 0), stop=(c == 0 and s == 3))
            last.then_inc(av_done, 1)

        @block.tensor
        def _(pe):
            with pe.Fori(0, NP) as hp:
                for step in range(K + LA):
                    if step < K:
                        scores(pe, hp, step)
                    if 0 <= step - LT < K:
                        transposes(pe, hp, step - LT)
                    if 0 <= step - LA < K:
                        values(pe, hp, step - LA)

        @block.scalar
        def _(act):
            for s in stored:
                act.sem_inc(s, 16)
            with act.Fori(0, NP) as hp:
                for step in range(K + LA + 2):
                    if step < K:
                        act.wait_ge(z_done, hp * K + step + 1)
                        act.wait_ge(scanned, hp * 2 * K + 2 * step + 2)
                        nc.scalar.activation(stay[:, step % 4, :], z[step % 2][:], ACT.Sigmoid,
                                             scale=-scale).then_inc(stay_ready, 1)
                    t = step - LT
                    if 0 <= t < K:
                        act.wait_ge(rt_done[0], 12 + hp * K + t + 1)
                        act.wait_ge(av_done, hp * K + t + 1)
                        nc.scalar.activation(RT[:, 0, t % 4, :], rt[0][:], ACT.Copy).then_inc(rt_copied[0], 1)
                    v = step - LA - 1
                    if v >= 0 and v % 4 == 3 and units[v // 4][1] == 0:
                        G = units[v // 4][0]
                        act.wait_ge(av_done, 4 + hp * K + v + 1)
                        act.wait_ge(stored[G % 2], hp * 16 * (NG // 2) + 16 * (G // 2) + 16)
                        nc.scalar.activation(stage[:, G % 2, :], out[G % 2][:], ACT.Identity,
                                             bias=k.v_last[:, bass.ds(hp * NG + G, 1)]).then_inc(out_copied, 1)
                        act.wait_ge(out_copied, 2 + hp * NG + G + 1)
                        act.dma_start(io.mix_t[bass.ds(hp * P, P), G * GT:(G + 1) * GT],
                                      stage[:, G % 2, :]).then_inc(stored[G % 2], 16)
            for s in stored:
                act.wait_ge(s, 16 * (NP * NG // 2 + 1))

        @block.vector
        def _(dve):
            dve.sem_inc(stay_ready, 2)
            dve.sem_inc(scanned, 8)
            dve.sem_inc(av_done, 4)
            dve.sem_inc(out_copied, 2)
            for h in range(2):
                dve.sem_inc(rt_done[h], 12)
                dve.sem_inc(rt_copied[h], 1)
            with dve.Fori(0, NP) as hp:
                for step in range(K + LT):
                    if step < K:
                        n, s = divmod(step, 4)
                        G, c = units[n]
                        h = s // 2
                        dve.wait_ge(stay_ready, 2 + hp * K + step + 1)
                        dve.wait_ge(rt_done[h], hp * K + 4 * n + 4)
                        for i in range(2):
                            qt = 2 * (s % 2) + i
                            if c == G:
                                initial = 1.0
                            else:
                                dve.wait_ge(scanned, 8 + hp * 8 * U + 8 * (n - 1) + 4 * h + qt + 1)
                                initial = R[:, (n - 1) % 3, h, qt, 0:1]
                            src = stay[:, step % 4, i * GT:(i + 1) * GT]
                            nc.vector.tensor_tensor_scan(R[:, n % 3, h, qt, ::-1], src[:, ::-1], src[:, ::-1],
                                                         initial, ALU.mult, ALU.bypass).then_inc(scanned, 1)
                    t = step - LT
                    if 0 <= t < K:
                        dve.wait_ge(rt_done[1], 12 + hp * K + t + 1)
                        dve.wait_ge(av_done, hp * K + t + 1)
                        nc.vector.tensor_copy(RT[:, 1, t % 4, :], rt[1][:]).then_inc(rt_copied[1], 1)


def mix(nc, k, io):
    with ExitStack() as outer:
        sb, ps, sem = alloc(nc, outer)
        w_hi = sb("mix_w_hi", [P, DC, D], F32R)
        w_lo = sb("mix_w_lo", [P, DC, D], F32R)
        split_weights(nc, io.w_out, D, w_hi, w_lo, sb, sem, "mix_", gain=k.g_mix)
        with ExitStack() as ctx:
            sb, ps, sem = alloc(nc, ctx)
            RING = 4
            NR = NGRP + NE
            w_router = sb("mix_w_router", [P, DC, NR])
            g_norm2 = sb("mix_g_norm2", [P, D])
            raw = sb("mix_raw", [P, RING, DC, P])
            hi = sb("mix_hi", [P, RING, DC, P], F32R)
            lo = sb("mix_lo", [P, RING, DC, P], F32R)
            sq = sb("mix_sq", [P, 2, DC, P])
            x = sb("mix_x", [P, RING, D])
            h = sb("mix_h", [P, RING, D])
            u2 = sb("mix_u2", [P, RING, D])
            u2_t = sb("mix_u2_t", [P, 2, DC, P])
            junk = sb("mix_junk", [P, D])
            rms, rinv = sb("mix_rms", [P, 2]), sb("mix_rinv", [P, 2])
            sum2, rms2, rinv2 = sb("mix_sum2", [P, 1]), sb("mix_rms2", [P, 1]), sb("mix_rinv2", [P, 1])
            half_out = [[ps(f"mix_out{half}{n}", [P, GT]) for n in range(2)] for half in range(2)]
            sums = ps("mix_sums", [P, 2])
            tr = [ps(f"mix_tr{i}", [P, GT]) for i in range(2)]
            logits = ps("mix_logits", [P, NR])
            params = sem("mix_params")
            raw_loaded = [sem(f"mix_raw_loaded{i}") for i in range(RING)]
            x_loaded = [sem(f"mix_x_loaded{i}") for i in range(RING)]
            hi_ready = sem("mix_hi_ready")
            sq_ready = sem("mix_sq_ready")
            lo_ready = sem("mix_lo_ready")
            sums_done = sem("mix_sums_done")
            rms_ready = sem("mix_rms_ready")
            rinv_ready = sem("mix_rinv_ready")
            first_done = sem("mix_first_done")
            second_done = sem("mix_second_done")
            half_ready = sem("mix_half_ready")
            h_ready = sem("mix_h_ready")
            squared = sem("mix_squared")
            rms2_ready = sem("mix_rms2_ready")
            rinv2_ready = sem("mix_rinv2_ready")
            u2_ready = sem("mix_u2_ready")
            u2_transposed = sem("mix_u2_transposed")
            u2_t_ready = sem("mix_u2_t_ready")
            logits_done = sem("mix_logits_done")
            logits_ready = sem("mix_logits_ready")
            stored = [sem(f"mix_stored{i}") for i in range(RING)]
            block = ctx.enter_context(nc.Block())

            def groups(engine, group):
                group(engine, 0, True, False)
                with engine.Fori(1, NG - 1) as G:
                    group(engine, G, False, False)
                group(engine, NG - 1, False, True)

            def load(sp, G, t):
                T = G * RING + t
                sp.dma_start(raw[:, t, :, :], io.mix_t[:, bass.ds(T * P, P)].rearrange("(c p) s -> p c s", p=P)
                             ).then_inc(raw_loaded[t], 16)
                sp.dma_start(x[:, t, :], io.x[bass.ds(T * P, P), :]).then_inc(x_loaded[t], 16)

            def sp_group(sp, G, first, last):
                for t in range(RING):
                    T = G * RING + t
                    hold(sp, k, h_ready, T * 2 + 4)
                    if not last:
                        load(sp, G + 1, t)
                    hold(sp, k, u2_ready, T + 2)
                    sp.dma_start(io.h[bass.ds(T * P, P), :], h[:, t, :]).then_inc(stored[t], 16)
                    sp.dma_start(io.u2[bass.ds(T * P, P), :], u2[:, t, :]).then_inc(stored[t], 16)

            @block.sync
            def _(sp):
                for s in stored:
                    sp.sem_inc(s, 32)
                sp.dma_start(g_norm2[:], io.norm2_g.unsqueeze(0).partition_broadcast(P)).then_inc(params, 16)
                with nc.allow_non_contiguous_dma(reason="router weights, once"):
                    sp.dma_start(w_router[:, :, 0:NGRP], io.w_group.rearrange("(c p) n -> p c n", p=P)).then_inc(params, 16)
                    sp.dma_start(w_router[:, :, NGRP:], io.w_fine.rearrange("(c p) n -> p c n", p=P)).then_inc(params, 16)
                for t in range(RING):
                    load(sp, 0, t)
                groups(sp, sp_group)
                for s in stored:
                    sp.wait_ge(s, 32 * (NG + 1))

            def pe_transposes(pe, T, t):
                pe.wait_ge(u2_ready, T + 2)
                pe.wait_ge(u2_t_ready, T + 1)
                for c in range(DC):
                    last = nc.tensor.transpose(tr[c // 4][:, (c % 4) * P:(c % 4 + 1) * P], u2[:, t, c * P:(c + 1) * P],
                                               k.ident[:])
                last.then_inc(u2_transposed, 1)

            def pe_logits(pe, T, t):
                pe.wait_ge(u2_t_ready, T + 2)
                pe.wait_ge(logits_ready, T + 1)
                for c in range(DC):
                    last = nc.tensor.matmul(logits[:], u2_t[:, t % 2, c, :], w_router[:, c, :],
                                            start=(c == 0), stop=(c == DC - 1))
                last.then_inc(logits_done, 1)

            def pe_group(pe, G, first, last):
                for t in range(RING):
                    T = G * RING + t
                    before = not (first and t == 0)
                    pe.wait_ge(sq_ready, T + 1)
                    pe.wait_ge(rms_ready, T + 1)
                    for half in range(2):
                        for c in range(NP):
                            end = nc.tensor.matmul(sums[:, half:half + 1], sq[:, t % 2, half * NP + c, :], k.ones[:],
                                                   start=(c == 0), stop=(c == NP - 1))
                    end.then_inc(sums_done, 1)
                    pe.wait_ge(lo_ready, T + 1)
                    for half in range(2):
                        for n in range(2):
                            pe.wait_ge((half_ready, h_ready)[half], T * 2 + n + 1)
                            for c in range(half * NP, half * NP + NP):
                                for m, (a, w) in enumerate(((hi, w_hi), (lo, w_hi), (hi, w_lo))):
                                    end = nc.tensor.matmul(half_out[half][n][:], a[:, t, c, :],
                                                           w[:, c, n * GT:(n + 1) * GT],
                                                           start=(c == half * NP and m == 0),
                                                           stop=(c == half * NP + NP - 1 and m == 2))
                            end.then_inc((first_done, second_done)[half], 1)
                        if half == 0 and before:
                            pe_transposes(pe, T - 1, (t - 1) % RING)
                    if before:
                        pe_logits(pe, T - 1, (t - 1) % RING)

            @block.tensor
            def _(pe):
                pe.wait_ge(params, 48)
                groups(pe, pe_group)
                pe_transposes(pe, NT - 1, RING - 1)
                pe_logits(pe, NT - 1, RING - 1)

            def act_inputs(act, G, t):
                T = G * RING + t
                act.wait_ge(raw_loaded[t], G * 16 + 16)
                act.wait_ge(second_done, T * 2 + 2)
                nc.scalar.activation(hi[:, t, :, :], raw[:, t, :, :], ACT.Copy).then_inc(hi_ready, 1)
                act.wait_ge(sums_done, T + 1)
                nc.scalar.activation(sq[:, t % 2, :, :], raw[:, t, :, :], ACT.Square).then_inc(sq_ready, 1)

            def act_u2_t(act, T, t):
                act.wait_ge(u2_transposed, T + 1)
                act.wait_ge(logits_done, T + 1)
                for i in range(2):
                    end = nc.scalar.activation(u2_t[:, t % 2, 4 * i:4 * i + 4, :], tr[i][:].rearrange("p (c n) -> p c n", c=4), ACT.Copy)
                end.then_inc(u2_t_ready, 1)

            def act_group(act, G, first, last):
                for t in range(RING):
                    T = G * RING + t
                    act.wait_ge(sums_done, T + 3)
                    act.wait_ge(rinv_ready, T + 1)
                    nc.scalar.activation(rms[:], sums[:], ACT.Sqrt, scale=1.0 / W_SB, bias=k.eps[:]).then_inc(rms_ready, 1)
                    if t < RING - 1:
                        act_inputs(act, G, t + 1)
                    elif not last:
                        act_inputs(act, G + 1, 0)
                    if not (first and t == 0):
                        act_u2_t(act, T - 1, (t - 1) % RING)
                    act.wait_ge(h_ready, T * 2 + 4)
                    act.wait_ge(rms2_ready, T + 1)
                    act.wait_ge(squared, T + 1)
                    nc.scalar.activation(junk[:], h[:, t, :], ACT.Square, accum_out=sum2[:]).then_inc(squared, 1)
                    act.wait_ge(squared, T + 2)
                    act.wait_ge(rinv2_ready, T + 1)
                    nc.scalar.activation(rms2[:], sum2[:], ACT.Sqrt, scale=1.0 / D, bias=k.eps[:]).then_inc(rms2_ready, 1)

            @block.scalar
            def _(act):
                act_inputs(act, 0, 0)
                groups(act, act_group)
                act_u2_t(act, NT - 1, RING - 1)

            def dve_low(dve, G, t):
                T = G * RING + t
                dve.wait_ge(hi_ready, T + 1)
                nc.vector.tensor_tensor(lo[:, t, :, :], raw[:, t, :, :], f32(hi[:, t, :, :]), ALU.subtract).then_inc(lo_ready, 1)

            def dve_logits(dve, T):
                dve.wait_ge(logits_done, T + 3)
                nc.vector.tensor_tensor(k.logits[:, bass.ds(T * NR, NR)], logits[:], k.b_router[:], ALU.add).then_inc(logits_ready, 1)

            def dve_group(dve, G, first, last):
                for t in range(RING):
                    T = G * RING + t
                    dve.wait_ge(rms_ready, T + 2)
                    dve.wait_ge(h_ready, T * 2 + 2)
                    nc.vector.reciprocal(rinv[:], rms[:]).then_inc(rinv_ready, 1)
                    dve.wait_ge(rinv_ready, T + 2)
                    dve.wait_ge(x_loaded[t], G * 16 + 16)
                    dve.wait_ge(stored[t], G * 32 + 32)
                    for n in range(2):
                        cols = slice(n * GT, (n + 1) * GT)
                        dve.wait_ge(first_done, T * 2 + n + 1)
                        nc.vector.scalar_tensor_tensor(h[:, t, cols], half_out[0][n][:], rinv[:, 0:1], x[:, t, cols],
                                                       ALU.mult, ALU.add).then_inc(half_ready, 1)
                    if t < RING - 1:
                        dve_low(dve, G, t + 1)
                    elif not last:
                        dve_low(dve, G + 1, 0)
                    for n in range(2):
                        cols = slice(n * GT, (n + 1) * GT)
                        dve.wait_ge(second_done, T * 2 + n + 1 + 2 * RING)
                        dve.wait_ge(half_ready, T * 2 + n + 3)
                        nc.vector.scalar_tensor_tensor(h[:, t, cols], half_out[1][n][:], rinv[:, 1:2], h[:, t, cols],
                                                       ALU.mult, ALU.add).then_inc(h_ready, 1)
                    if not (first and t == 0):
                        dve_logits(dve, T - 1)
                    dve.wait_ge(rms2_ready, T + 2)
                    dve.wait_ge(u2_ready, T + 1)
                    nc.vector.reciprocal(rinv2[:], rms2[:]).then_inc(rinv2_ready, 1)
                    dve.wait_ge(rinv2_ready, T + 2)
                    nc.vector.scalar_tensor_tensor(u2[:, t, :], h[:, t, :], rinv2[:], g_norm2[:],
                                                   ALU.mult, ALU.mult).then_inc(u2_ready, 1)

            @block.vector
            def _(dve):
                for s, start in ((sums_done, 2), (rms_ready, 1), (rinv_ready, 1), (second_done, 2 * RING),
                                 (half_ready, 2), (h_ready, 2), (squared, 1), (rms2_ready, 1), (rinv2_ready, 1),
                                 (u2_ready, 1), (u2_t_ready, 1), (logits_done, 2), (logits_ready, 1)):
                    dve.sem_inc(s, start)
                dve.wait_ge(params, 48)
                dve_low(dve, 0, 0)
                groups(dve, dve_group)
                dve_logits(dve, NT - 1)


def route(nc, k, io):
    with ExitStack() as ctx:
        sb, ps, sem = alloc(nc, ctx)
        NR = NGRP + NE
        iota_i = sb("rt_iota_i", [P, WIDE], I32)
        iota = sb("rt_iota", [P, WIDE])
        ids = sb("rt_ids", [P, NT], I32)
        zeros = sb("rt_zeros", [P, WIDE], I32)
        small = lambda name, *shape: sb("rt_" + name, [P, NT, *shape])
        g_max, g_dist, g_exp, g_sum, g_prob = small("g_max"), small("g_dist", NGRP), small("g_exp", NGRP), small("g_sum"), small("g_prob")
        g_eq, g_cand, g_first, g_hot, g_pen = small("g_eq", NGRP), small("g_cand", NGRP), small("g_first"), small("g_hot", NGRP), small("g_pen", NGRP)
        fine = [small(f"fine{i}", NE) for i in range(TOPK)]
        top, first = [small(f"top{i}") for i in range(TOPK)], [small(f"first{i}") for i in range(TOPK)]
        hot = [small(f"hot{i}", NE) for i in range(TOPK)]
        eq, cand = small("eq", NE), small("cand", NE)
        dist, ratio, denom, share = small("dist"), small("ratio"), small("denom"), small("share")
        both = sb("rt_both", [P, NT * NE], BF16)
        seg = sb("rt_seg", [P, NE, NT])
        totals, upto, base = (sb("rt_" + n, [P, NE, NT]) for n in ("totals", "upto", "base"))
        slot_all = small("slot_all", NE)
        picked = small("picked", NE)
        slot_f = small("slot_f")
        count_f, tiles_f, end_f, start_f, ones_e = (sb("rt_" + n, [P, NE]) for n in ("count_f", "tiles_f", "end_f", "start_f", "ones_e"))
        count_i = sb("rt_count_i", [P, NE], I32)
        tiles_i = sb("rt_tiles_i", [P, NE], I32)
        lane_i, lane_f, row_i, row_f, where_f = sb("rt_lane_i", [P, NT], I32), small("lane_f"), sb("rt_row_i", [P, NT], I32), small("row_f"), small("where_f")
        where = sb("rt_where", [P, TOPK, NT], I32)
        below = sb("rt_below", [1, WIDE, NE])
        expert_f = sb("rt_expert_f", [1, WIDE])
        pairs_i, pairs_f = sb("rt_pairs_i", [1, 1], I32), sb("rt_pairs_f", [1, 1])
        prefix = [ps(f"rt_prefix{i}", [P, GT]) for i in range(2)]
        total = [ps(f"rt_total{i}", [P, GT]) for i in range(2)]
        iota_ready, step, g_exp_ready, ratio_ready = sem("rt_iota_ready"), sem("rt_step"), sem("rt_g_exp_ready"), sem("rt_ratio_ready")
        counted, zeros_stored = sem("rt_counted"), sem("rt_zeros_stored")
        g_dist_ready, dist_ready, both_ready, where_ready = sem("rt_g_dist_ready"), sem("rt_dist_ready"), sem("rt_both_ready"), sem("rt_where_ready")
        logits = k.logits[:].rearrange("p (t n) -> p t n", n=NR)
        block = ctx.enter_context(nc.Block())

        def spread(ap, n):
            return ap.unsqueeze(2).to_broadcast([P, NT, n])

        def along(n):
            return iota[:, 0:n].unsqueeze(1).to_broadcast([P, NT, n])

        @block.gpsimd
        def _(pool):
            nc.gpsimd.iota(iota_i[:], pattern=[[1, WIDE]], base=0, channel_multiplier=0)
            nc.gpsimd.iota(ids[:], pattern=[[P, NT]], base=0, channel_multiplier=1)
            nc.gpsimd.memset(zeros[:], 0)
            nc.gpsimd.memset(ones_e[:], 1.0)
            nc.gpsimd.memset(seg[:], 1.0).then_inc(iota_ready, 1)
            pool.wait_ge(iota_ready, 1)
            nc.gpsimd.memset(seg[:, :, 0:1], 0.0).then_inc(iota_ready, 1)
            pool.wait_ge(zeros_stored, 16)
            pool.wait_ge(where_ready, TOPK)
            for c in range(TOPK):
                for t in range(NT):
                    pool.indirect_dma_start(out=io.slot_token, out_offset=bass.IndirectOffsetOnAxis(ap=where[:, c, t:t + 1], axis=0),
                                            in_=ids[:, t:t + 1], in_offset=None).then_inc(k.scattered, 16)
            pool.wait_ge(k.scattered, 16 * TOPK * NT)

        @block.sync
        def _(sp):
            sp.wait_ge(iota_ready, 1)
            sp.dma_start(io.slot_token.rearrange("(p t) o -> p (t o)", p=P), zeros[:]).then_inc(zeros_stored, 16)
            sp.wait_ge(zeros_stored, 16)

        @block.scalar
        def _(act):
            act.wait_ge(g_dist_ready, 1)
            nc.scalar.activation(g_exp[:], g_dist[:], ACT.Exp).then_inc(g_exp_ready, 1)
            act.wait_ge(dist_ready, 1)
            nc.scalar.activation(ratio[:], dist[:], ACT.Exp).then_inc(ratio_ready, 1)

        @block.tensor
        def _(pe):
            pe.wait_ge(both_ready, 1)
            for i in range(2):
                nc.tensor.matmul(prefix[i][:], k.before[:], both[:, i * GT:(i + 1) * GT], start=True, stop=True)
            for i in range(2):
                last = nc.tensor.matmul(total[i][:], k.ones_bf[:], both[:, i * GT:(i + 1) * GT], start=True, stop=True)
            last.then_inc(counted, 1)

        @block.vector
        def _(dve):
            count = [0]

            def link(instruction):
                count[0] += 1
                instruction.then_inc(step, 1)
                dve.wait_ge(step, count[0])

            def done(sem_ready):
                dve.sem_inc(sem_ready, 1)

            V = nc.vector
            dve.wait_ge(iota_ready, 2)
            link(V.tensor_copy(iota[:], iota_i[:]))
            g_logits = logits[:, :, 0:NGRP]
            link(V.tensor_reduce(g_max[:], g_logits, AX.X, ALU.max))
            link(V.tensor_tensor(g_dist[:], g_logits, spread(g_max[:], NGRP), ALU.subtract))
            done(g_dist_ready)
            link(V.tensor_scalar(g_eq[:], g_dist[:], 0.0, None, ALU.is_equal))
            link(V.scalar_tensor_tensor(g_cand[:], g_eq[:], -2.0 * NE, along(NGRP), ALU.mult, ALU.add))
            link(V.tensor_reduce(g_first[:], g_cand[:], AX.X, ALU.min))
            link(V.tensor_tensor(g_hot[:], g_cand[:], spread(g_first[:], NGRP), ALU.is_equal))
            link(V.tensor_scalar(g_pen[:], g_hot[:], -MASKED, MASKED, ALU.mult, ALU.add))
            link(V.tensor_tensor(fine[0][:].rearrange("p t (g e) -> p t g e", g=NGRP),
                                 logits[:, :, NGRP:].rearrange("p t (g e) -> p t g e", g=NGRP),
                                 g_pen[:].unsqueeze(3).to_broadcast([P, NT, NGRP, EPG]), ALU.add))
            for c in range(TOPK):
                link(V.tensor_reduce(top[c][:], fine[c][:], AX.X, ALU.max))
                link(V.tensor_tensor(eq[:], fine[c][:], spread(top[c][:], NE), ALU.is_equal))
                link(V.scalar_tensor_tensor(cand[:], eq[:], -2.0 * NE, along(NE), ALU.mult, ALU.add))
                link(V.tensor_reduce(first[c][:], cand[:], AX.X, ALU.min))
                link(V.tensor_tensor(hot[c][:], cand[:], spread(first[c][:], NE), ALU.is_equal))
                if c == 0:
                    link(V.scalar_tensor_tensor(fine[1][:], hot[0][:], 3 * MASKED, fine[0][:], ALU.mult, ALU.add))
            link(V.tensor_tensor(both[:].rearrange("p (t e) -> p t e", e=NE), hot[0][:], hot[1][:], ALU.add))
            done(both_ready)
            link(V.tensor_tensor(dist[:], top[1][:], top[0][:], ALU.subtract))
            done(dist_ready)
            dve.wait_ge(g_exp_ready, 1)
            link(V.tensor_reduce(g_sum[:], g_exp[:], AX.X, ALU.add))
            link(V.reciprocal(g_prob[:], g_sum[:]))
            dve.wait_ge(ratio_ready, 1)
            link(V.tensor_scalar(denom[:], ratio[:], 1.0, None, ALU.add))
            link(V.reciprocal(share[:], denom[:]))
            link(V.tensor_tensor(k.weight[:, 0, :], share[:], g_prob[:], ALU.mult))
            link(V.tensor_tensor(k.weight[:, 1, :], k.weight[:, 0, :], ratio[:], ALU.mult))
            dve.wait_ge(counted, 1)
            for i in range(2):
                half = NT // 2
                link(V.tensor_copy(totals[:, :, i * half:(i + 1) * half], total[i][:].rearrange("p (t e) -> p e t", e=NE)))
            flat = lambda ap: ap[:].rearrange("p e t -> p (e t)")
            link(V.tensor_tensor_scan(flat(upto), flat(seg), flat(totals), 0.0, ALU.mult, ALU.add))
            link(V.tensor_tensor(base[:], upto[:], totals[:], ALU.subtract))
            link(V.tensor_scalar(count_f[:], upto[:, :, NT - 1], float(P - 1), None, ALU.add))
            link(V.tensor_copy(count_i[:], count_f[:]))
            link(V.tensor_scalar(tiles_i[:], count_i[:], 7, None, ALU.logical_shift_right))
            link(V.tensor_copy(tiles_f[:], tiles_i[:]))
            link(V.tensor_tensor_scan(end_f[:], ones_e[:], tiles_f[:], 0.0, ALU.mult, ALU.add))
            link(V.tensor_tensor(start_f[:], end_f[:], tiles_f[:], ALU.subtract))
            link(V.scalar_tensor_tensor(base[:], start_f[:].unsqueeze(2).to_broadcast([P, NE, NT]), float(P), base[:], ALU.mult, ALU.add))
            for i in range(2):
                half = NT // 2
                link(V.tensor_tensor(slot_all[:, i * half:(i + 1) * half, :], prefix[i][:].rearrange("p (t e) -> p t e", e=NE),
                                     base[:, :, i * half:(i + 1) * half].rearrange("p e t -> p t e"), ALU.add))
            for c in range(TOPK):
                link(V.tensor_tensor(picked[:], slot_all[:], hot[c][:], ALU.mult))
                link(V.tensor_reduce(slot_f[:], picked[:], AX.X, ALU.add))
                link(V.tensor_copy(k.slot[:, c, :], slot_f[:]))
                link(V.tensor_scalar(lane_i[:], k.slot[:, c, :], P - 1, None, ALU.bitwise_and))
                link(V.tensor_scalar(row_i[:], k.slot[:, c, :], 7, None, ALU.logical_shift_right))
                link(V.tensor_copy(lane_f[:], lane_i[:]))
                link(V.tensor_copy(row_f[:], row_i[:]))
                link(V.scalar_tensor_tensor(where_f[:], lane_f[:], float(WIDE), row_f[:], ALU.mult, ALU.add))
                link(V.tensor_copy(where[:, c, :], where_f[:]))
                done(where_ready)
            link(V.tensor_tensor(below[:], end_f[0:1, :].unsqueeze(1).to_broadcast([1, WIDE, NE]),
                                 iota[0:1, :].unsqueeze(2).to_broadcast([1, WIDE, NE]), ALU.is_le))
            link(V.tensor_reduce(expert_f[:], below[:], AX.X, ALU.add))
            link(V.tensor_scalar(expert_f[:], expert_f[:], float(NE - 1), None, ALU.min))
            link(V.tensor_copy(k.tile_expert[:], expert_f[:]))
            link(V.tensor_scalar(k.tile_buffer[:], k.tile_expert[:], 1, None, ALU.bitwise_and))
            link(V.tensor_copy(k.expert_end[:], end_f[0:1, :]))
            link(V.tensor_scalar(pairs_f[:], end_f[0:1, NE - 1:NE], 1.0, None, ALU.add))
            link(V.tensor_copy(pairs_i[:], pairs_f[:]))
            link(V.tensor_scalar(k.tile_pairs[:], pairs_i[:], 1, None, ALU.logical_shift_right))


def experts(nc, k, io):
    with ExitStack() as ctx:
        sb, ps, sem = alloc(nc, ctx)
        WG, WD = DC * DE, FC * D
        w_gate = sb("ex_w_gate", [P, 2 * WG])
        w_up = sb("ex_w_up", [P, 2 * WG])
        w_down = sb("ex_w_down", [P, 2 * WD])
        ids = sb("ex_ids", [P, WIDE], I32)
        index = sb("ex_index", [P, 2], I32)
        xg = sb("ex_xg", [P, 2, D])
        x_t = sb("ex_x_t", [P, 2, DC, P])
        silu = sb("ex_silu", [P, DE])
        hidden = sb("ex_hidden", [P, DE])
        hidden_t = sb("ex_hidden_t", [P, FC, P])
        y = sb("ex_y", [P, 2, D])
        gate, up, h_tr = ps("ex_gate", [P, DE]), ps("ex_up", [P, DE]), ps("ex_h_tr", [P, DE])
        x_tr = [ps(f"ex_x_tr{i}", [P, GT]) for i in range(2)]
        down = [ps(f"ex_down{i}", [P, GT]) for i in range(2)]
        index_ready = sem("ex_index_ready")
        gathered = k.x_gathered
        w_loaded = sem("ex_w_loaded")
        x_transposed = sem("ex_x_transposed")
        x_t_ready = [sem(f"ex_x_t_ready{i}") for i in range(2)]
        gate_done, up_done = sem("ex_gate_done"), sem("ex_up_done")
        silu_ready = sem("ex_silu_ready")
        hidden_ready = sem("ex_hidden_ready")
        h_transposed = sem("ex_h_transposed")
        hidden_t_ready = sem("ex_hidden_t_ready")
        down_first = sem("ex_down_first")
        tiles_done = sem("ex_tiles_done")
        y_ready = [sem(f"ex_y_ready{i}") for i in range(2)]
        y_stored = [sem(f"ex_y_stored{i}") for i in range(2)]
        block = ctx.enter_context(nc.Block())
        most = MAX_TILES // 2

        def pairs(engine):
            return engine.value_load(k.tile_pairs[0:1, 0:1], min_val=1, max_val=most)

        def load_weights(sp, e, b):
            one = lambda w: w[bass.ds(e, 1)].rearrange("e (c p) n -> p (e c) n", p=P)
            for dst, src, n in ((w_gate, io.w_e_gate, WG), (w_up, io.w_e_up, WG), (w_down, io.w_e_down, WD)):
                c = DC if n == WG and dst is not w_down else FC
                sp.dma_start(dst[:, b * n:(b + 1) * n].rearrange("p (c n) -> p c n", c=c), one(src)).then_inc(w_loaded, 16)

        @block.sync
        def _(sp):
            for b in range(2):
                load_weights(sp, b, b)
                sp.wait_ge(w_loaded, 48 * (b + 1))
            with sp.Fori(1, NE // 2) as i:
                for b in range(2):
                    last_tile = sp.value_load(k.expert_end[0:1, bass.ds(i * 2 + (b - 2), 1)], min_val=0, max_val=MAX_TILES)
                    hold(sp, k, tiles_done, last_tile + 1)
                    load_weights(sp, i * 2 + b, b)
                    hold(sp, k, w_loaded, i * 96 + 48 * (b + 1))

        @block.gpsimd
        def _(pool):
            pool.dma_start(ids[:], io.slot_token.rearrange("(p t) o -> p (t o)", p=P)).then_inc(k.ids_loaded, 16)
            pool.wait_ge(k.ids_loaded, 16)

            def gather(T, u, n):
                pool.wait_ge(x_transposed, T)
                nc.gpsimd.tensor_copy(index[:, u:u + 1], ids[:, bass.ds(T, 1)]).then_inc(index_ready, 1)
                hold(pool, k, index_ready, T + 1)
                pool.indirect_dma_start(out=xg[:, u, :], out_offset=None, in_=io.u2,
                                        in_offset=bass.IndirectOffsetOnAxis(ap=index[:, u:u + 1], axis=0)).then_inc(gathered[u], 16)

            nc.gpsimd.tensor_copy(index[:, 0:1], ids[:, 0:1]).then_inc(index_ready, 1)
            pool.wait_ge(index_ready, 1)
            pool.indirect_dma_start(out=xg[:, 0, :], out_offset=None, in_=io.u2,
                                    in_offset=bass.IndirectOffsetOnAxis(ap=index[:, 0:1], axis=0)).then_inc(gathered[0], 16)
            with pool.Fori(0, pairs(pool)) as i:
                for u in range(2):
                    gather(i * 2 + (u + 1), (u + 1) % 2, i)

        def pe_transpose(pe, T, u, n):
            pe.wait_ge(gathered[u], n * 16 + 16)
            for half in range(2):
                pe.wait_ge(x_t_ready[half], T + 1)
                for c in range(4):
                    last = nc.tensor.transpose(x_tr[half][:, c * P:(c + 1) * P],
                                               xg[:, u, (4 * half + c) * P:(4 * half + c + 1) * P], k.ident[:])
            last.then_inc(x_transposed, 1)

        @block.tensor
        def _(pe):
            pe_transpose(pe, 0, 0, 0)
            with pe.Fori(0, pairs(pe)) as i:
                for u in range(2):
                    T = i * 2 + u
                    e = pe.value_load(k.tile_expert[0:1, bass.ds(T, 1)], min_val=0, max_val=NE - 1)
                    b = pe.value_load(k.tile_buffer[0:1, bass.ds(T, 1)], min_val=0, max_val=1)
                    pe.wait_ge(w_loaded, e * 48 + 48)
                    for half in range(2):
                        pe.wait_ge(x_t_ready[half], T + 2)
                    pe.wait_ge(hidden_ready, T + 1)
                    for w, dst, done in ((w_gate, gate, gate_done), (w_up, up, up_done)):
                        for c in range(DC):
                            last = nc.tensor.matmul(dst[:], x_t[:, u, c, :], w[:, bass.ds(b * WG + c * DE, DE)],
                                                    start=(c == 0), stop=(c == DC - 1))
                        last.then_inc(done, 1)
                    pe_transpose(pe, T + 1, (u + 1) % 2, i + u)
                    pe.wait_ge(hidden_ready, T + 2)
                    for f in range(FC):
                        last = nc.tensor.transpose(h_tr[:, f * P:(f + 1) * P], hidden[:, f * P:(f + 1) * P], k.ident[:])
                    last.then_inc(h_transposed, 1)
                    pe.wait_ge(hidden_t_ready, T + 1)
                    for n in range(2):
                        pe.wait_ge(y_ready[n], T + 1)
                        for f in range(FC):
                            last = nc.tensor.matmul(down[n][:], hidden_t[:, f, :], w_down[:, bass.ds(b * WD + f * D + n * GT, GT)],
                                                    start=(f == 0), stop=(f == FC - 1))
                        last.then_inc((down_first, tiles_done)[n], 1)

        def copy_x_t(engine, copy, T, u, half):
            engine.wait_ge(x_transposed, T + 2)
            copy(x_t[:, u, 4 * half:4 * half + 4, :], x_tr[half][:].rearrange("p (c n) -> p c n", c=4)).then_inc(x_t_ready[half], 1)

        act_copy = lambda out, in_: nc.scalar.activation(out, in_, ACT.Copy)
        dve_copy = lambda out, in_: nc.vector.tensor_copy(out, in_)

        @block.scalar
        def _(act):
            for s in y_stored:
                act.sem_inc(s, 16)
            copy_x_t(act, act_copy, 0, 0, 0)
            with act.Fori(0, pairs(act)) as i:
                for u in range(2):
                    T = i * 2 + u
                    act.wait_ge(gate_done, T + 1)
                    act.wait_ge(hidden_ready, T + 1)
                    nc.scalar.activation(silu[:], gate[:], ACT.Silu).then_inc(silu_ready, 1)
                    act.wait_ge(tiles_done, T + 1)
                    copy_x_t(act, act_copy, T + 1, (u + 1) % 2, 0)
                    act.wait_ge(h_transposed, T + 2)
                    act.wait_ge(tiles_done, T + 1)
                    nc.scalar.activation(hidden_t[:], h_tr[:].rearrange("p (f n) -> p f n", f=FC), ACT.Copy).then_inc(hidden_t_ready, 1)
                    act.wait_ge(down_first, T + 1)
                    act.wait_ge(y_stored[u], i * 16 + 16)
                    nc.scalar.activation(y[:, u, 0:GT], down[0][:], ACT.Copy).then_inc(y_ready[0], 1)
                    for half in range(2):
                        act.wait_ge(y_ready[half], T + 2)
                    act.dma_start(io.ys[bass.ds(T * P, P), :], y[:, u, :]).then_inc(y_stored[u], 16)
            n = pairs(act)
            for s in y_stored:
                hold(act, k, s, n * 16 + 16)

        @block.vector
        def _(dve):
            dve.sem_inc(x_transposed, 1)
            dve.sem_inc(hidden_ready, 1)
            dve.sem_inc(h_transposed, 1)
            dve.sem_inc(tiles_done, 1)
            for half in range(2):
                dve.sem_inc(x_t_ready[half], 1)
                dve.sem_inc(y_ready[half], 1)
            copy_x_t(dve, dve_copy, 0, 0, 1)
            with dve.Fori(0, pairs(dve)) as i:
                for u in range(2):
                    T = i * 2 + u
                    dve.wait_ge(silu_ready, T + 1)
                    dve.wait_ge(up_done, T + 1)
                    dve.wait_ge(h_transposed, T + 1)
                    nc.vector.tensor_tensor(hidden[:], silu[:], up[:], ALU.mult).then_inc(hidden_ready, 1)
                    dve.wait_ge(tiles_done, T + 1)
                    copy_x_t(dve, dve_copy, T + 1, (u + 1) % 2, 1)
                    dve.wait_ge(tiles_done, T + 2)
                    dve.wait_ge(y_stored[u], i * 16 + 16)
                    nc.vector.tensor_copy(y[:, u, GT:D], down[1][:]).then_inc(y_ready[1], 1)


def combine(nc, k, io):
    with ExitStack() as ctx:
        sb, ps, sem = alloc(nc, ctx)
        RING = 4
        g_final = sb("co_g_final", [P, D])
        index = sb("co_index", [P, RING, TOPK], I32)
        h = sb("co_h", [P, RING, D])
        ye = sb("co_ye", [P, RING, TOPK, D])
        acc = sb("co_acc", [P, RING, D])
        out = sb("co_out", [P, RING, D])
        junk = sb("co_junk", [P, D])
        total, rms, rinv = sb("co_total", [P, 1]), sb("co_rms", [P, 1]), sb("co_rinv", [P, 1])
        params = sem("co_params")
        h_loaded = [sem(f"co_h_loaded{i}") for i in range(RING)]
        gathered = k.y_gathered
        index_ready, acc_ready = sem("co_index_ready"), sem("co_acc_ready")
        sum_ready = sem("co_sum_ready")
        rms_ready, rinv_ready, out_ready = sem("co_rms_ready"), sem("co_rinv_ready"), sem("co_out_ready")
        squared = sem("co_squared")
        stored = [sem(f"co_stored{i}") for i in range(RING)]
        block = ctx.enter_context(nc.Block())

        def groups(engine, group):
            group(engine, 0, True, False)
            with engine.Fori(1, NG - 1) as G:
                group(engine, G, False, False)
            group(engine, NG - 1, False, True)

        def load(sp, G, t):
            sp.dma_start(h[:, t, :], io.h[bass.ds(G * GT + t * P, P), :]).then_inc(h_loaded[t], 16)

        def sp_group(sp, G, first, last):
            for t in range(RING):
                T = G * RING + t
                hold(sp, k, sum_ready, T * 2 + 2)
                if not last:
                    load(sp, G + 1, t)
                hold(sp, k, out_ready, T + 2)
                sp.dma_start(io.out[bass.ds(T * P, P), :], out[:, t, :]).then_inc(stored[t], 16)

        @block.sync
        def _(sp):
            for s in stored:
                sp.sem_inc(s, 16)
            sp.dma_start(g_final[:], io.final_g.unsqueeze(0).partition_broadcast(P)).then_inc(params, 16)
            for t in range(RING):
                load(sp, 0, t)
            groups(sp, sp_group)
            for s in stored:
                sp.wait_ge(s, 16 * (NG + 1))

        def pool_group(pool, G, first, last):
            for t in range(RING):
                T = G * RING + t
                if not first:
                    pool.wait_ge(sum_ready, T * 2 + 2 - 2 * RING)
                for c in range(TOPK):
                    nc.gpsimd.tensor_copy(index[:, t, c:c + 1], k.slot[:, c, bass.ds(T, 1)]).then_inc(index_ready, 1)
                hold(pool, k, index_ready, T * 2 + 2)
                for c in range(TOPK):
                    pool.indirect_dma_start(out=ye[:, t, c, :], out_offset=None, in_=io.ys,
                                            in_offset=bass.IndirectOffsetOnAxis(ap=index[:, t, c:c + 1], axis=0)).then_inc(gathered[t], 16)

        @block.gpsimd
        def _(pool):
            groups(pool, pool_group)

        def act_group(act, G, first, last):
            for t in range(RING):
                T = G * RING + t
                act.wait_ge(sum_ready, T * 2 + 2)
                act.wait_ge(rms_ready, T + 1)
                act.wait_ge(squared, T + 1)
                nc.scalar.activation(junk[:], acc[:, t, :], ACT.Square, accum_out=total[:]).then_inc(squared, 1)
                act.wait_ge(squared, T + 2)
                act.wait_ge(rinv_ready, T + 1)
                nc.scalar.activation(rms[:], total[:], ACT.Sqrt, scale=1.0 / D, bias=k.eps[:]).then_inc(rms_ready, 1)

        @block.scalar
        def _(act):
            groups(act, act_group)

        def dve_group(dve, G, first, last):
            for t in range(RING):
                T = G * RING + t
                dve.wait_ge(h_loaded[t], G * 16 + 16)
                dve.wait_ge(gathered[t], G * 32 + 32)
                dve.wait_ge(out_ready, T + 1)
                nc.vector.scalar_tensor_tensor(acc[:, t, :], ye[:, t, 0, :], k.weight[:, 0, bass.ds(T, 1)], h[:, t, :],
                                               ALU.mult, ALU.add).then_inc(sum_ready, 1)
                dve.wait_ge(sum_ready, T * 2 + 1)
                nc.vector.scalar_tensor_tensor(acc[:, t, :], ye[:, t, 1, :], k.weight[:, 1, bass.ds(T, 1)], acc[:, t, :],
                                               ALU.mult, ALU.add).then_inc(sum_ready, 1)
                dve.wait_ge(rms_ready, T + 2)
                nc.vector.reciprocal(rinv[:], rms[:]).then_inc(rinv_ready, 1)
                dve.wait_ge(rinv_ready, T + 2)
                dve.wait_ge(stored[t], G * 16 + 16)
                nc.vector.scalar_tensor_tensor(out[:, t, :], acc[:, t, :], rinv[:], g_final[:],
                                               ALU.mult, ALU.mult).then_inc(out_ready, 1)

        @block.vector
        def _(dve):
            for s in (squared, rms_ready, rinv_ready, out_ready):
                dve.sem_inc(s, 1)
            dve.wait_ge(params, 16)
            groups(dve, dve_group)


class Names:
    pass


def build(nc, io):
    scratch = lambda name, shape, dt=F32: nc.dram_tensor("s_" + name, shape, dt, kind="Internal").ap()
    io.q_hi, io.q_lo = scratch("q_hi", [W_SB, S]), scratch("q_lo", [W_SB, S])
    io.k_hi, io.k_lo = scratch("k_hi", [W_SB, S]), scratch("k_lo", [W_SB, S])
    io.dv = scratch("dv", [S, W_SB])
    io.mix_t = scratch("mix_t", [D, S])
    io.h = scratch("h", [S, D])
    io.u2 = scratch("u2", [S, D])
    io.slot_token = scratch("slot_token", [WIDE * P, 1], I32)
    io.ys = scratch("ys", [MAX_TILES * P, D])
    with ExitStack() as ctx:
        sb, ps, sem = alloc(nc, ctx)
        k = Names()
        k.passed = sem("passed")
        k.spare_filled, k.scattered, k.ids_loaded = sem("spare_filled"), sem("scattered"), sem("ids_loaded")
        k.x_gathered = [sem(f"x_gathered{i}") for i in range(2)]
        k.y_gathered = [sem(f"y_gathered{i}") for i in range(4)]
        k.ident, k.ident_r, k.ident_bf = sb("ident", [P, P]), sb("ident_r", [P, P], F32R), sb("ident_bf", [P, P], BF16)
        k.before, k.ones_bf, k.ones = sb("before", [P, P], BF16), sb("ones_bf", [P, P], BF16), sb("ones", [P, 1])
        k.mask = sb("mask", [P, TT, GT], BF16)
        k.g_norm1, k.g_mix = sb("g_norm1", [P, DC]), sb("g_mix", [P, DC])
        k.conv_b, k.conv_w = sb("conv_b", [P, NL]), sb("conv_w", [P, CONV, NL])
        k.b_r, k.b_i, k.lam = sb("b_r", [P, NL]), sb("b_i", [P, NL]), sb("lam", [P, NL])
        k.b_router = sb("b_router", [P, NGRP + NE])
        k.v_last = sb("v_last", [P, NP * NG])
        k.eps = sb("eps", [P, 1])
        constants(nc, k, io)
        for stage in (qkv, lru, attention):
            stage(nc, k, io)
        k.logits = sb("logits", [P, NT * (NGRP + NE)])
        k.weight = sb("weight", [P, TOPK, NT])
        k.slot = sb("slot", [P, TOPK, NT], I32)
        k.tile_expert, k.tile_buffer = sb("tile_expert", [1, WIDE], I32), sb("tile_buffer", [1, WIDE], I32)
        k.expert_end, k.tile_pairs = sb("expert_end", [1, NE], I32), sb("tile_pairs", [1, 1], I32)
        for stage in (mix, route, experts, combine):
            stage(nc, k, io)


INPUTS = ["x", "norm1_g", "w_in", "conv_w", "conv_b", "w_rgate", "b_rgate", "w_igate", "b_igate", "lam",
          "sb_norm_g", "lru_norm_g", "w_out", "norm2_g", "w_group", "b_group", "w_fine", "b_fine",
          "w_e_gate", "w_e_up", "w_e_down", "final_g"]


def kernel(**inputs):
    import concourse.bacc as bacc
    from concourse.bass_utils import run_bass_kernel_spmd

    nc = bacc.Bacc("TRN2", target_bir_lowering=False, num_devices=1)
    io, arrays = Names(), {}
    batch = inputs["x"].shape[0]
    for name in INPUTS:
        a = np.ascontiguousarray(inputs[name])
        if name == "x":
            a = a.reshape(batch * S, D)
        arrays["in_" + name] = a
        ap = nc.dram_tensor("in_" + name, a.shape, mybir.dt.from_np(a.dtype), kind="ExternalInput").ap()
        io.__dict__[name] = ap
    io.out = nc.dram_tensor("out", (batch * S, D), F32, kind="ExternalOutput").ap()
    build(nc, io)
    result = run_bass_kernel_spmd(nc, [arrays], core_ids=[0])
    return result.results[0]["out"].reshape(batch, S, D)
```

```python
from contextlib import ExitStack

import numpy as np

import concourse.bass as bass
from concourse import mybir

F32 = mybir.dt.float32
F32R = mybir.dt.float32r
BF16 = mybir.dt.bfloat16
I32 = mybir.dt.int32
U32 = mybir.dt.uint32
ALU = mybir.AluOpType
ACT = mybir.ActivationFunctionType
AX = mybir.AxisListType

P = 128
D = 1024
S = 4096
DC = D // P
GT = 512
NG = S // GT
TT = GT // P
NT = S // P
HD = 64
W_SB = 512
W_LRU = 512
NP = W_SB // P
NL = W_LRU // P
CONV = 4
RG_C = 8.0
EPS = 1e-6
NGRP = 4
EPG = 8
NE = NGRP * EPG
DE = 512
FC = DE // P
TOPK = 2
MAX_TILES = S * TOPK // P + NE
WIDE = MAX_TILES + 2
MATRICES = 3
WM = D * DE // P
PIECES = 4
MASKED = -1e30


def alloc(nc, ctx):
    held = []

    def sem(name):
        held.append(nc.alloc_semaphore(name))
        return held[-1]

    def clear():
        if held:
            nc.clear_and_free_semaphores(held)
            nc.all_engine_barrier()

    ctx.callback(clear)
    sb = lambda name, shape, dt=F32: ctx.enter_context(nc.sbuf_tensor(name, shape, dt))
    ps = lambda name, shape, dt=F32: ctx.enter_context(nc.psum_tensor(name, shape, dt))
    return sb, ps, sem


def hold(engine, k, semaphore, value):
    engine.wait_ge(semaphore, value)
    engine.sem_inc(k.passed, 1)


def f32(ap):
    return ap.bitcast(F32)


def constants(nc, k, io):
    with ExitStack() as ctx:
        sb, ps, sem = alloc(nc, ctx)
        filled, selected, loaded = sem("c_filled"), sem("c_selected"), sem("c_loaded")
        block = ctx.enter_context(nc.Block())

        @block.gpsimd
        def _(pool):
            nc.gpsimd.memset(k.ident[:], 0.0)
            nc.gpsimd.memset(k.ident_bf[:], 0.0)
            nc.gpsimd.memset(k.before[:], 1.0)
            nc.gpsimd.memset(k.ones_bf[:], 1.0)
            nc.gpsimd.memset(k.ones[:], 1.0)
            nc.gpsimd.memset(k.eps[:], EPS)
            nc.gpsimd.memset(k.mask[:], 0.0).then_inc(filled, 1)
            pool.wait_ge(filled, 1)
            for m in (k.ident, k.ident_bf):
                nc.gpsimd.affine_select(out=m[:], in_=m[:], compare_op=ALU.not_equal, fill=1.0, base=0,
                                        pattern=[[-1, P]], channel_multiplier=1)
            nc.gpsimd.affine_select(out=k.before[:], in_=k.before[:], compare_op=ALU.is_gt, fill=0.0, base=0,
                                    pattern=[[1, P]], channel_multiplier=-1)
            nc.gpsimd.affine_select(out=k.mask[:], in_=k.mask[:], compare_op=ALU.is_gt, fill=MASKED, base=0,
                                    pattern=[[-1, P]], channel_multiplier=1).then_inc(selected, 1)
            pool.wait_ge(selected, 1)

        @block.sync
        def _(sp):
            with nc.allow_non_contiguous_dma(reason="parameters of a few KB, once"):
                col = lambda v: v.rearrange("(c p) -> p c", p=P)
                for dst, src in ((k.g_norm1, io.norm1_g), (k.g_mix[:, 0:NP], io.sb_norm_g),
                                 (k.g_mix[:, NP:2 * NP], io.lru_norm_g), (k.conv_b, io.conv_b),
                                 (k.b_r, io.b_rgate), (k.b_i, io.b_igate), (k.lam, io.lam)):
                    sp.dma_start(dst[:], col(src)).then_inc(loaded, 16)
                sp.dma_start(k.conv_w[:], io.conv_w.rearrange("t (c p) -> p t c", p=P)).then_inc(loaded, 16)
            for dst, src in ((k.b_router[:, 0:NGRP], io.b_group), (k.b_router[:, NGRP:], io.b_fine)):
                sp.dma_start(dst, src.unsqueeze(0).partition_broadcast(P)).then_inc(loaded, 16)
            sp.wait_ge(loaded, 10 * 16)

        @block.vector
        def _(dve):
            dve.wait_ge(selected, 1)
            nc.vector.tensor_copy(k.ident_r[:], k.ident[:]).then_inc(filled, 1)
            dve.wait_ge(filled, 2)


class NormedGroups:

    def __init__(self, nc, k, io, sb, ps, sem, tag):
        self.nc, self.k, self.io = nc, k, io
        self.x = sb(tag + "x", [P, TT, D])
        self.junk = sb(tag + "junk", [P, D])
        self.sumsq = sb(tag + "sumsq", [P, TT])
        self.rms = sb(tag + "rms", [P, TT])
        self.rinv = sb(tag + "rinv", [P, TT])
        self.hi = sb(tag + "u_hi", [P, DC, GT], F32R)
        self.lo = sb(tag + "u_lo", [P, DC, GT], F32R)
        self.tr = [ps(f"{tag}tr{i}", [P, GT]) for i in range(2)]
        self.x_loaded = [sem(f"{tag}x_loaded{t}") for t in range(TT)]
        self.squared = sem(tag + "squared")
        self.rms_ready = sem(tag + "rms_ready")
        self.rinv_ready = sem(tag + "rinv_ready")
        self.x_scaled = sem(tag + "x_scaled")
        self.transposed = sem(tag + "transposed")
        self.hi_ready = sem(tag + "hi_ready")
        self.lo_ready = sem(tag + "lo_ready")

    def load(self, sp, G):
        for t in range(TT):
            sp.dma_start(self.x[:, t, :], self.io.x[bass.ds(G * GT + t * P, P), :]).then_inc(self.x_loaded[t], 16)

    def load_after(self, sp, G):
        hold(sp, self.k, self.transposed, G * DC + DC)
        self.load(sp, G + 1)

    def norm(self, act, G):
        nc = self.nc
        for t in range(TT):
            act.wait_ge(self.x_loaded[t], G * 16 + 16)
            if t > 0:
                act.wait_ge(self.squared, G * TT + t)
            nc.scalar.activation(self.junk[:], self.x[:, t, :], ACT.Square,
                                 accum_out=self.sumsq[:, t:t + 1]).then_inc(self.squared, 1)
        act.wait_ge(self.squared, G * TT + TT)
        nc.scalar.activation(self.rms[:], self.sumsq[:], ACT.Sqrt, scale=1.0 / D,
                             bias=self.k.eps[:]).then_inc(self.rms_ready, 1)

    def scale(self, dve, G):
        nc = self.nc
        dve.wait_ge(self.rms_ready, G + 1)
        nc.vector.reciprocal(self.rinv[:], self.rms[:]).then_inc(self.rinv_ready, 1)
        dve.wait_ge(self.rinv_ready, G + 1)
        for t in range(TT):
            nc.vector.tensor_scalar(self.x[:, t, :], self.x[:, t, :], self.rinv[:, t:t + 1], None,
                                    ALU.mult).then_inc(self.x_scaled, 1)

    def transpose(self, pe, G, c):
        nc = self.nc
        if c == 0:
            pe.wait_ge(self.x_scaled, G * TT + TT)
        pe.wait_ge(self.lo_ready, G * DC + c + 1)
        for t in range(TT):
            last = nc.tensor.transpose(self.tr[c % 2][:, t * P:(t + 1) * P], self.x[:, t, c * P:(c + 1) * P],
                                       self.k.ident[:])
        last.then_inc(self.transposed, 1)

    def high(self, act, G):
        nc = self.nc
        for c in range(DC):
            act.wait_ge(self.transposed, G * DC + c + 1)
            nc.scalar.activation(self.hi[:, c, :], self.tr[c % 2][:], ACT.Copy,
                                 scale=self.k.g_norm1[:, c:c + 1]).then_inc(self.hi_ready, 1)

    def low(self, dve, G):
        nc = self.nc
        for c in range(DC):
            dve.wait_ge(self.hi_ready, G * DC + c + 1)
            nc.vector.scalar_tensor_tensor(self.lo[:, c, :], self.tr[c % 2][:], self.k.g_norm1[:, c:c + 1],
                                           f32(self.hi[:, c, :]), ALU.mult, ALU.subtract).then_inc(self.lo_ready, 1)

    def product(self, pe, G, bank, weights, col, chunks):
        nc = self.nc
        for c in chunks:
            pe.wait_ge(self.lo_ready, G * DC + c + 3)
            for n, (w, u) in enumerate(((weights.hi, self.hi), (weights.hi, self.lo), (weights.lo, self.hi))):
                last = nc.tensor.matmul(bank[:], w[:, c, col:col + P], u[:, c, :],
                                        start=(c == 0 and n == 0), stop=(c == DC - 1 and n == 2))
        return last

    def leading_product(self, pe, G, bank, weights, col):
        self.transpose(pe, G, 0)
        self.transpose(pe, G, 1)
        for c in range(DC):
            pe.wait_ge(weights.low_ready, c + 1)
            last = self.product(pe, G, bank, weights, col, [c])
            if c + 2 < DC:
                self.transpose(pe, G, c + 2)
        return last


class SplitWeights:

    def __init__(self, nc, src, cols, sb, sem, tag, gain=None):
        self.nc, self.src, self.gain = nc, src, gain
        self.hi = sb(tag + "w_hi", [P, DC, cols], F32R)
        self.lo = sb(tag + "w_lo", [P, DC, cols], F32R)
        self.raw = sb(tag + "w_raw", [P, 2, cols])
        self.arrived = [sem(f"{tag}w_arrived{i}") for i in range(2)]
        self.high_ready = sem(tag + "w_high_ready")
        self.low_ready = sem(tag + "w_low_ready")

    def load(self, sp):
        for c in range(DC):
            if c >= 2:
                sp.wait_ge(self.low_ready, c - 1)
            sp.dma_start(self.raw[:, c % 2, :], self.src[c * P:(c + 1) * P, :]).then_inc(self.arrived[c % 2], 16)

    def factor(self, c):
        return 1.0 if self.gain is None else self.gain[:, c:c + 1]

    def high(self, act):
        for c in range(DC):
            act.wait_ge(self.arrived[c % 2], 16 * (c // 2 + 1))
            self.nc.scalar.activation(self.hi[:, c, :], self.raw[:, c % 2, :], ACT.Copy,
                                      scale=self.factor(c)).then_inc(self.high_ready, 1)

    def low(self, dve):
        for c in range(DC):
            dve.wait_ge(self.high_ready, c + 1)
            self.nc.vector.scalar_tensor_tensor(self.lo[:, c, :], self.raw[:, c % 2, :], self.factor(c),
                                                f32(self.hi[:, c, :]), ALU.mult, ALU.subtract).then_inc(self.low_ready, 1)


def qkv(nc, k, io):
    with ExitStack() as outer:
        sb, ps, sem = alloc(nc, outer)
        weights = SplitWeights(nc, io.w_in[:, 0:3 * W_SB], 3 * W_SB, sb, sem, "qkv_")
        with ExitStack() as ctx:
            sb, ps, sem = alloc(nc, ctx)
            ug = NormedGroups(nc, k, io, sb, ps, sem, "qkv_")
            out = [ps(f"qkv_out{i}", [P, GT]) for i in range(4)]
            dv_tr = [ps(f"qkv_dv_tr{i}", [P, GT]) for i in range(2)]
            st_hi = [sb(f"qkv_st_hi{i}", [P, GT], F32R) for i in range(4)]
            st_lo = [sb(f"qkv_st_lo{i}", [P, GT], F32R) for i in range(4)]
            v = sb("qkv_v", [P, NP, GT + 1])
            dv = sb("qkv_dv", [P, NP, GT])
            st_dv = [sb(f"qkv_st_dv{i}", [P, GT]) for i in range(2)]
            v_done = sem("qkv_v_done")
            v_copied = sem("qkv_v_copied")
            v_zeroed = sem("qkv_v_zeroed")
            dv_ready = sem("qkv_dv_ready")
            v_carried = sem("qkv_v_carried")
            dv_transposed = sem("qkv_dv_transposed")
            dv_staged = sem("qkv_dv_staged")
            dv_stored = [sem(f"qkv_dv_stored{i}") for i in range(2)]
            qk_done = sem("qkv_qk_done")
            qk_high = sem("qkv_qk_high")
            qk_low = sem("qkv_qk_low")
            qk_stored = [sem(f"qkv_qk_stored{i}") for i in range(4)]
            zeros = sb("qkv_zeros", [P, D])
            cleared = sem("qkv_cleared")
            block = ctx.enter_context(nc.Block())

            @block.gpsimd
            def _(pool):
                nc.gpsimd.memset(zeros[:], 0.0).then_inc(cleared, 1)
                pool.wait_ge(cleared, 1)
                pool.wait_ge(weights.low_ready, DC)
                with pool.Fori(S * TOPK // P, MAX_TILES) as T:
                    pool.dma_start(io.ys[bass.ds(T * P, P), :], zeros[:]).then_inc(k.spare_filled, 16)
                pool.wait_ge(k.spare_filled, 16 * (MAX_TILES - S * TOPK // P))

            @block.tensor
            def _(pe):
                with pe.Fori(0, NG) as G:
                    for j in range(NP):
                        pe.wait_ge(qk_low, G * 8 + j + 1)
                        if j == 0:
                            last = ug.leading_product(pe, G, out[0], weights, 2 * W_SB)
                        else:
                            last = ug.product(pe, G, out[j], weights, 2 * W_SB + j * P, range(DC))
                        last.then_inc(v_done, 1)
                    for j in range(NP):
                        pe.wait_ge(v_copied, G * NP + j + 1)
                        ug.product(pe, G, out[j], weights, j * P, range(DC)).then_inc(qk_done, 1)
                    for j in range(NP):
                        pe.wait_ge(dv_ready, G * NP + j + 1)
                        pe.wait_ge(dv_staged, G * NP + j + 1)
                        for b in range(TT):
                            last = nc.tensor.transpose(dv_tr[j % 2][:, b * P:(b + 1) * P],
                                                       dv[:, j, b * P:(b + 1) * P], k.ident[:])
                        last.then_inc(dv_transposed, 1)
                    for j in range(NP):
                        pe.wait_ge(qk_low, G * 8 + j + 5)
                        ug.product(pe, G, out[j], weights, W_SB + j * P, range(DC)).then_inc(qk_done, 1)

            def split_high(act, G, m):
                act.wait_ge(qk_done, G * 8 + m + 1)
                act.wait_ge(qk_stored[m % 4], G * 64 + (m // 4) * 32 + 32)
                nc.scalar.activation(st_hi[m % 4][:], out[m % 4][:], ACT.Copy).then_inc(qk_high, 1)

            def act_group(act, G, last):
                ug.high(act, G)
                for j in range(NP):
                    act.wait_ge(v_done, G * NP + j + 1)
                    act.wait_ge(v_carried, G * NP + j + 1)
                    nc.scalar.activation(v[:, j, 1:GT + 1], out[j][:], ACT.Copy).then_inc(v_copied, 1)
                    if j == 1 and not last:
                        ug.norm(act, G + 1)
                for m in range(4):
                    split_high(act, G, m)
                for j in range(NP):
                    act.wait_ge(dv_transposed, G * NP + j + NP + 1)
                    act.wait_ge(dv_stored[j % 2], G * 32 + (j // 2) * 16 + 16)
                    nc.scalar.activation(st_dv[j % 2][:], dv_tr[j % 2][:], ACT.Copy).then_inc(dv_staged, 1)
                for m in range(4, 8):
                    split_high(act, G, m)

            @block.scalar
            def _(act):
                ug.norm(act, 0)
                weights.high(act)
                with act.Fori(0, NG - 1) as G:
                    act_group(act, G, False)
                act_group(act, NG - 1, True)

            def split_low(dve, G, m):
                dve.wait_ge(qk_high, G * 8 + m + 1)
                nc.vector.tensor_tensor(st_lo[m % 4][:], out[m % 4][:], f32(st_hi[m % 4][:]),
                                        ALU.subtract).then_inc(qk_low, 1)

            def dve_group(dve, G, last):
                ug.low(dve, G)
                for j in range(NP):
                    dve.wait_ge(v_copied, G * NP + j + 1)
                    dve.wait_ge(dv_transposed, G * NP + j + 1)
                    nc.vector.tensor_tensor(dv[:, j, :], v[:, j, 0:GT], v[:, j, 1:GT + 1],
                                            ALU.subtract).then_inc(dv_ready, 1)
                    nc.vector.tensor_copy(k.v_last[:, bass.ds(G * TT + j * NT, TT)], v[:, j, P::P])
                    dve.wait_ge(dv_ready, G * NP + j + 1)
                    nc.vector.tensor_copy(v[:, j, 0:1], v[:, j, GT:GT + 1]).then_inc(v_carried, 1)
                    if j == 1 and not last:
                        ug.scale(dve, G + 1)
                for m in range(8):
                    split_low(dve, G, m)

            @block.vector
            def _(dve):
                nc.vector.memset(v[:], 0.0).then_inc(v_zeroed, 1)
                dve.wait_ge(v_zeroed, 1)
                dve.sem_inc(v_carried, NP)
                dve.sem_inc(ug.lo_ready, 2)
                dve.sem_inc(qk_low, 4)
                dve.sem_inc(dv_transposed, NP)
                dve.sem_inc(dv_staged, 2)
                ug.scale(dve, 0)
                weights.low(dve)
                with dve.Fori(0, NG - 1) as G:
                    dve_group(dve, G, False)
                dve_group(dve, NG - 1, True)

            def store_qk(sp, G, m):
                dst_hi, dst_lo = (io.q_hi, io.q_lo) if m < 4 else (io.k_hi, io.k_lo)
                hold(sp, k, qk_low, G * 8 + m + 5)
                rows = slice((m % 4) * P, (m % 4 + 1) * P)
                sp.dma_start(dst_hi[rows, bass.ds(G * GT, GT)], f32(st_hi[m % 4][:])).then_inc(qk_stored[m % 4], 16)
                sp.dma_start(dst_lo[rows, bass.ds(G * GT, GT)], f32(st_lo[m % 4][:])).then_inc(qk_stored[m % 4], 16)

            def sp_group(sp, G, last):
                if not last:
                    ug.load_after(sp, G)
                for m in range(4):
                    store_qk(sp, G, m)
                for j in range(NP):
                    hold(sp, k, dv_staged, G * NP + j + 3)
                    dst = io.dv[bass.ds(G * GT, GT), j * P:(j + 1) * P].rearrange("(b p) c -> p b c", p=P)
                    sp.dma_start(dst, st_dv[j % 2][:].rearrange("p (b c) -> p b c", b=TT)).then_inc(dv_stored[j % 2], 16)
                for m in range(4, 8):
                    store_qk(sp, G, m)

            @block.sync
            def _(sp):
                for s in qk_stored:
                    sp.sem_inc(s, 32)
                for s in dv_stored:
                    sp.sem_inc(s, 16)
                ug.load(sp, 0)
                weights.load(sp)
                with sp.Fori(0, NG - 1) as G:
                    sp_group(sp, G, False)
                sp_group(sp, NG - 1, True)
                for s in qk_stored:
                    sp.wait_ge(s, 32 * (2 * NG + 1))
                for s in dv_stored:
                    sp.wait_ge(s, 16 * (2 * NG + 1))


def lru(nc, k, io):
    with ExitStack() as outer:
        sb, ps, sem = alloc(nc, outer)
        weights = SplitWeights(nc, io.w_in[:, 3 * W_SB:], 2 * W_LRU, sb, sem, "lru_")
        gates = sb("lru_gates", [P, 2, NL, P])
        slope = sb("lru_slope", [P, NL])
        neg_slope = sb("lru_neg_slope", [P, NL])
        with ExitStack() as ctx:
            sb, ps, sem = alloc(nc, ctx)
            e, w, w2, acc, relu = (sb("lru_lam_" + n, [P, NL]) for n in ("e", "w", "w2", "acc", "relu"))
            cleared, gates_loaded = sem("lru_cleared"), sem("lru_gates_loaded")
            exp_ready, step, slope_ready = sem("lru_exp_ready"), sem("lru_step"), sem("lru_slope_ready")
            ug = NormedGroups(nc, k, io, sb, ps, sem, "lru_")
            out = [ps(f"lru_out{i}", [P, GT]) for i in range(4)]
            gate_out = [ps(f"lru_gate_out{i}", [P, GT]) for i in range(2)]
            H = CONV - 1
            xl = sb("lru_xl", [P, NL, GT + H])
            xc = sb("lru_xc", [P, 2, NL, GT])
            gelu = sb("lru_gelu", [P, NL, GT])
            r = sb("lru_r", [P, NL, GT])
            ig = sb("lru_ig", [P, NL, GT])
            a = sb("lru_a", [P, NL, GT])
            th = sb("lru_th", [P, NL, GT])
            sq = sb("lru_sq", [P, NL, GT])
            h = r
            state = sb("lru_state", [P, NL])
            x_done = sem("lru_x_done")
            x_copied = sem("lru_x_copied")
            x_carried = sem("lru_x_carried")
            g_done = sem("lru_g_done")
            g_ready = sem("lru_g_ready")
            conv_step = sem("lru_conv_step")
            xc_ready = sem("lru_xc_ready")
            gate_done = sem("lru_gate_done")
            r_ready = sem("lru_r_ready")
            i_ready = sem("lru_i_ready")
            ix_ready = sem("lru_ix_ready")
            a_ready = sem("lru_a_ready")
            th_ready = sem("lru_th_ready")
            sq_ready = sem("lru_sq_ready")
            m2_ready = sem("lru_m2_ready")
            m_ready = sem("lru_m_ready")
            in_ready = sem("lru_in_ready")
            h_ready = sem("lru_h_ready")
            state_ready = sem("lru_state_ready")
            out_ready = sem("lru_out_ready")
            stored = [sem(f"lru_stored{j}") for j in range(NL)]
            zeroed = sem("lru_zeroed")
            block = ctx.enter_context(nc.Block())

            def sp_group(sp, G, last):
                if not last:
                    ug.load_after(sp, G)

            def sp_stores(sp, G):
                for j in range(NL):
                    hold(sp, k, out_ready, G * NL + j + NL + 1)
                    sp.dma_start(io.mix_t[W_SB + j * P:W_SB + (j + 1) * P, bass.ds(G * GT, GT)],
                                 sq[:, j, :]).then_inc(stored[j], 16)

            @block.sync
            def _(sp):
                for s in stored:
                    sp.sem_inc(s, 16)
                ug.load(sp, 0)
                sp.wait_ge(cleared, 1)
                for n, src in enumerate((io.w_rgate, io.w_igate)):
                    for half in range(2):
                        lanes = slice(64 * half, 64 * half + 64)
                        sp.dma_start(gates[lanes, n, :, 64 * half:64 * half + 64],
                                     src.rearrange("(j half) c d -> half c j d", half=2)[half]).then_inc(gates_loaded, 16)
                weights.load(sp)
                sp_group(sp, 0, False)
                with sp.Fori(1, NG - 1) as G:
                    sp_group(sp, G, False)
                    sp_stores(sp, G - 1)
                sp_stores(sp, NG - 2)
                sp_stores(sp, NG - 1)
                for s in stored:
                    sp.wait_ge(s, 16 * (NG + 1))

            @block.tensor
            def _(pe):
                pe.wait_ge(gates_loaded, 64)
                with pe.Fori(0, NG) as G:
                    for j in range(NL):
                        pe.wait_ge(g_ready, G * NL + j + 1)
                        if j == 0:
                            last = ug.leading_product(pe, G, out[0], weights, 0)
                        else:
                            last = ug.product(pe, G, out[j], weights, j * P, range(DC))
                        last.then_inc(x_done, 1)
                    for j in range(NL):
                        pe.wait_ge(x_copied, G * NL + j + 1)
                        ug.product(pe, G, out[j], weights, W_LRU + j * P, range(DC)).then_inc(g_done, 1)
                    for j in range(NL):
                        pe.wait_ge(xc_ready, G * NL + j + 1)
                        for n, free in enumerate((r_ready, i_ready)):
                            pe.wait_ge(free, G * NL + j + 1)
                            nc.tensor.matmul(gate_out[n][:], gates[:, n, j, :], xc[:, 1, j, :],
                                             start=True, stop=True).then_inc(gate_done, 1)

            def act_middle(act, G, last):
                for j in range(NL):
                    act.wait_ge(x_done, G * NL + j + 1)
                    act.wait_ge(x_carried, G * NL + j + 1)
                    nc.scalar.activation(xl[:, j, H:], out[j][:], ACT.Copy).then_inc(x_copied, 1)
                if not last:
                    ug.norm(act, G + 1)
                for j in range(NL):
                    act.wait_ge(g_done, G * NL + j + 1)
                    act.wait_ge(out_ready, G * NL + j + 1)
                    nc.scalar.activation(gelu[:, j, :], out[j][:], ACT.Gelu_apprx_tanh).then_inc(g_ready, 1)
                for j in range(NL):
                    act.wait_ge(gate_done, G * 2 * NL + 2 * j + 1)
                    nc.scalar.activation(r[:, j, :], gate_out[0][:], ACT.Sigmoid,
                                         bias=k.b_r[:, j:j + 1]).then_inc(r_ready, 1)
                    act.wait_ge(gate_done, G * 2 * NL + 2 * j + 2)
                    act.wait_ge(in_ready, G * NL + j + 1)
                    nc.scalar.activation(ig[:, j, :], gate_out[1][:], ACT.Sigmoid,
                                         bias=k.b_i[:, j:j + 1]).then_inc(i_ready, 1)

            def act_tail(act, G):
                for j in range(NL):
                    act.wait_ge(r_ready, G * NL + j + 2)
                    act.wait_ge(h_ready, G * NL + j + 1)
                    nc.scalar.activation(a[:, j, :], r[:, j, :], ACT.Exp, scale=slope[:, j:j + 1]).then_inc(a_ready, 1)
                    act.wait_ge(in_ready, G * NL + j + 1)
                    nc.scalar.activation(th[:, j, :], r[:, j, :], ACT.Tanh,
                                         scale=neg_slope[:, j:j + 1]).then_inc(th_ready, 1)
                for j in range(NL):
                    act.wait_ge(m2_ready, G * NL + j + 1)
                    nc.scalar.activation(th[:, j, :], th[:, j, :], ACT.Sqrt).then_inc(m_ready, 1)

            @block.scalar
            def _(act):
                act.wait_ge(step, 2)
                nc.scalar.activation(e[:], relu[:], ACT.Exp, scale=-1.0).then_inc(exp_ready, 1)
                ug.norm(act, 0)
                weights.high(act)
                ug.high(act, 0)
                act_middle(act, 0, False)
                act.wait_ge(slope_ready, 1)
                with act.Fori(1, NG - 1) as G:
                    ug.high(act, G)
                    act_tail(act, G - 1)
                    act_middle(act, G, False)
                ug.high(act, NG - 1)
                act_tail(act, NG - 2)
                act_middle(act, NG - 1, True)
                act_tail(act, NG - 1)

            def dve_middle(dve, G, last):
                for j in range(NL):
                    dve.wait_ge(x_copied, G * NL + j + 1)
                    dve.wait_ge(ix_ready, G * NL + j + 1)
                    nc.vector.tensor_scalar(xc[:, 0, j, :], xl[:, j, H:H + GT], k.conv_w[:, H, j:j + 1],
                                            k.conv_b[:, j:j + 1], ALU.mult, ALU.add).then_inc(conv_step, 1)
                    for n, tap in enumerate(range(H - 1, -1, -1)):
                        dve.wait_ge(conv_step, (G * NL + j) * H + n + 1)
                        last_step = nc.vector.scalar_tensor_tensor(
                            xc[:, (n + 1) % 2, j, :], xl[:, j, tap:tap + GT], k.conv_w[:, tap, j:j + 1],
                            xc[:, n % 2, j, :], ALU.mult, ALU.add)
                        last_step.then_inc(conv_step if tap else xc_ready, 1)
                    dve.wait_ge(xc_ready, G * NL + j + 1)
                    nc.vector.tensor_copy(xl[:, j, 0:H], xl[:, j, GT:GT + H]).then_inc(x_carried, 1)
                if not last:
                    ug.scale(dve, G + 1)
                for j in range(NL):
                    dve.wait_ge(i_ready, G * NL + j + 2)
                    nc.vector.tensor_tensor(ig[:, j, :], ig[:, j, :], xc[:, 1, j, :], ALU.mult).then_inc(ix_ready, 1)

            def dve_tail(dve, G):
                for j in range(NL):
                    dve.wait_ge(th_ready, G * NL + j + NL + 1)
                    dve.wait_ge(sq_ready, G * NL + j + 1)
                    nc.vector.scalar_tensor_tensor(th[:, j, :], sq[:, j, :], 1.0, th[:, j, :], ALU.add,
                                                   ALU.mult).then_inc(m2_ready, 1)
                for j in range(NL):
                    dve.wait_ge(in_ready, G * NL + j + NL + 1)
                    dve.wait_ge(state_ready, G * NL + j + 1)
                    dve.wait_ge(out_ready, G * NL + j + 1)
                    nc.vector.tensor_tensor_scan(h[:, j, :], a[:, j, :], sq[:, j, :], state[:, j:j + 1],
                                                 ALU.mult, ALU.add).then_inc(h_ready, 1)
                for j in range(NL):
                    dve.wait_ge(h_ready, G * NL + j + NL + 1)
                    nc.vector.tensor_copy(state[:, j:j + 1], h[:, j, GT - 1:GT]).then_inc(state_ready, 1)
                    nc.vector.tensor_tensor(sq[:, j, :], h[:, j, :], gelu[:, j, :], ALU.mult).then_inc(out_ready, 1)

            def dve_slope(dve):
                count = [0]

                def link(instruction):
                    count[0] += 1
                    instruction.then_inc(step, 1)
                    dve.wait_ge(step, count[0])

                link(nc.vector.tensor_scalar(w[:], k.lam[:], -1.0, None, ALU.mult))
                link(nc.vector.tensor_tensor(relu[:], k.lam[:], w[:], ALU.max))
                dve.wait_ge(exp_ready, 1)
                link(nc.vector.tensor_scalar(w[:], e[:], 2.0, None, ALU.add))
                link(nc.vector.reciprocal(w2[:], w[:]))
                link(nc.vector.tensor_tensor(w[:], w2[:], e[:], ALU.mult))
                link(nc.vector.tensor_tensor(w2[:], w[:], w[:], ALU.mult))
                terms = 10
                link(nc.vector.memset(acc[:], 1.0 / (2 * terms + 1)))
                for n in range(terms - 1, -1, -1):
                    link(nc.vector.tensor_tensor(e[:], acc[:], w2[:], ALU.mult))
                    link(nc.vector.tensor_scalar(acc[:], e[:], 1.0 / (2 * n + 1), None, ALU.add))
                link(nc.vector.tensor_tensor(e[:], acc[:], w[:], ALU.mult))
                link(nc.vector.tensor_scalar(w[:], e[:], -2.0 * RG_C, None, ALU.mult))
                link(nc.vector.tensor_scalar(relu[:], k.lam[:], 0.0, RG_C, ALU.min, ALU.mult))
                link(nc.vector.tensor_tensor(slope[:], relu[:], w[:], ALU.add))
                link(nc.vector.tensor_scalar(neg_slope[:], slope[:], -1.0, None, ALU.mult))
                dve.sem_inc(slope_ready, 1)

            @block.vector
            def _(dve):
                dve_slope(dve)
                nc.vector.memset(xl[:], 0.0).then_inc(zeroed, 1)
                nc.vector.memset(state[:], 0.0).then_inc(zeroed, 1)
                dve.wait_ge(zeroed, 2)
                dve.sem_inc(x_carried, NL)
                dve.sem_inc(state_ready, NL)
                dve.sem_inc(ug.lo_ready, 2)
                dve.sem_inc(g_ready, NL)
                dve.sem_inc(out_ready, NL)
                dve.sem_inc(r_ready, 1)
                dve.sem_inc(i_ready, 1)
                dve.sem_inc(th_ready, NL)
                dve.sem_inc(h_ready, NL)
                dve.sem_inc(in_ready, NL)
                dve.sem_inc(ix_ready, NL)
                ug.scale(dve, 0)
                weights.low(dve)
                ug.low(dve, 0)
                dve_middle(dve, 0, False)
                with dve.Fori(1, NG - 1) as G:
                    ug.low(dve, G)
                    dve_tail(dve, G - 1)
                    dve_middle(dve, G, False)
                ug.low(dve, NG - 1)
                dve_tail(dve, NG - 2)
                dve_middle(dve, NG - 1, True)
                dve_tail(dve, NG - 1)

            @block.gpsimd
            def _(pool):
                nc.gpsimd.memset(gates[:], 0.0).then_inc(cleared, 1)
                with pool.Fori(0, NG) as G:
                    for j in range(NL):
                        pool.wait_ge(a_ready, G * NL + j + 1)
                        pool.wait_ge(stored[j], G * 16 + 16)
                        nc.gpsimd.tensor_tensor(sq[:, j, :], a[:, j, :], a[:, j, :], ALU.mult).then_inc(sq_ready, 1)
                    for j in range(NL):
                        pool.wait_ge(m_ready, G * NL + j + 1)
                        pool.wait_ge(ix_ready, G * NL + j + NL + 1)
                        nc.gpsimd.tensor_tensor(sq[:, j, :], th[:, j, :], ig[:, j, :], ALU.mult).then_inc(in_ready, 1)


def attention(nc, k, io):
    units = [(G, c) for G in range(NG) for c in range(G, -1, -1)]
    U = len(units)
    K = 4 * U
    LT = 6
    LA = LT + 1
    scale = HD ** -0.5
    with ExitStack() as ctx:
        sb, ps, sem = alloc(nc, ctx)
        q = sb("att_q", [P, 2, S], F32R)
        k_hi = sb("att_k_hi", [P, 2, S], F32R)
        k_lo = sb("att_k_lo", [P, 2, S], F32R)
        dv = sb("att_dv", [P, NT, P])
        stay = sb("att_stay", [P, 4, 2 * GT])
        R = sb("att_R", [P, 3, 2, TT, GT])
        RT = sb("att_RT", [P, 2, 4, GT])
        stage = sb("att_stage", [P, 2, GT])
        z = [ps(f"att_z{i}", [P, 2 * GT]) for i in range(2)]
        rt = [ps(f"att_rt{i}", [P, GT]) for i in range(2)]
        out = [ps(f"att_out{i}", [P, GT]) for i in range(2)]
        chunk_loaded = [sem(f"att_chunk_loaded{g}") for g in range(NG)]
        z_done = sem("att_z_done")
        stay_ready = sem("att_stay_ready")
        scanned = sem("att_scanned")
        rt_done = [sem(f"att_rt_done{h}") for h in range(2)]
        rt_copied = [sem(f"att_rt_copied{h}") for h in range(2)]
        av_done = sem("att_av_done")
        out_copied = sem("att_out_copied")
        stored = [sem(f"att_stored{i}") for i in range(2)]
        LOADS = 7
        block = ctx.enter_context(nc.Block())

        def load_rows(sp, hp, g, dst, src_low, src_high):
            cols = slice(g * GT, (g + 1) * GT)
            for lanes, src in ((slice(0, HD), src_low), (slice(HD, P), src_high)):
                sp.dma_start(f32(dst[lanes, :, cols]), src[bass.ds(hp * P, P), cols].rearrange("(h p) s -> p h s", h=2)
                             ).then_inc(chunk_loaded[g], 16)

        def load_queries(sp, hp, g):
            load_rows(sp, hp, g, q, io.q_hi, io.q_lo)

        def load_keys(sp, hp, g):
            load_rows(sp, hp, g, k_hi, io.k_hi, io.k_hi)
            load_rows(sp, hp, g, k_lo, io.k_lo, io.k_lo)
            cols = slice(g * GT, (g + 1) * GT)
            sp.dma_start(dv[:, g * TT:(g + 1) * TT, :],
                         io.dv[cols, bass.ds(hp * P, P)].rearrange("(t p) c -> p t c", p=P)).then_inc(chunk_loaded[g], 16)

        @block.sync
        def _(sp):
            for g in range(NG):
                load_queries(sp, 0, g)
                load_keys(sp, 0, g)
            with sp.Fori(1, NP) as hp:
                for g in range(NG - 1, -1, -1):
                    hold(sp, k, av_done, 4 + (hp - 1) * K + 4 * (units.index((NG - 1, g)) + 1))
                    load_keys(sp, hp, g)
                    if g < NG - 1:
                        load_queries(sp, hp, g)
                load_queries(sp, hp, NG - 1)

        def keys_of(c, G, qt):
            return (qt + 1) * P if c == G else GT

        def query_start(c, G, s):
            return s * P if c == G else 0

        def scores(pe, hp, step):
            n, s = divmod(step, 4)
            G, c = units[n]
            h = s // 2
            if s == 0 and c == G:
                pe.wait_ge(chunk_loaded[G], hp * 16 * LOADS + 16 * LOADS)
            pe.wait_ge(stay_ready, hp * K + step + 1)
            for i in range(2):
                qt = 2 * (s % 2) + i
                width = keys_of(c, G, qt)
                bank = z[step % 2][:, i * GT:i * GT + width]
                q_tile = q[:, h, G * GT + qt * P:G * GT + (qt + 1) * P]
                keys = slice(c * GT, c * GT + width)
                nc.tensor.matmul(bank, q_tile, k_hi[:, h, keys], start=True, stop=False)
                if c == G:
                    nc.tensor.matmul(bank[:, width - P:width], k.ident_bf[:], k.mask[:], start=False, stop=False)
                last = nc.tensor.matmul(bank, q_tile, k_lo[:, h, keys], start=False, stop=True)
            last.then_inc(z_done, 1)

        def transposes(pe, hp, step):
            n, s = divmod(step, 4)
            G, c = units[n]
            for h in range(2):
                pe.wait_ge(scanned, 8 + hp * 8 * U + 8 * n + 4 * h + 4)
                pe.wait_ge(rt_copied[h], hp * K + step + 1)
                for qt in range(query_start(c, G, s) // P, TT):
                    last = nc.tensor.transpose(rt[h][:, qt * P:(qt + 1) * P], R[:, n % 3, h, qt, s * P:(s + 1) * P],
                                               k.ident[:])
                last.then_inc(rt_done[h], 1)

        def values(pe, hp, step):
            n, s = divmod(step, 4)
            G, c = units[n]
            if c == G and s == 0:
                pe.wait_ge(out_copied, hp * NG + G + 1)
            for h in range(2):
                pe.wait_ge(rt_copied[h], hp * K + step + 2)
            queries = slice(query_start(c, G, s), GT)
            for h in range(2):
                last = nc.tensor.matmul(out[G % 2][h * HD:(h + 1) * HD, queries], dv[:, c * TT + s, h * HD:(h + 1) * HD],
                                        RT[:, h, s, queries], start=(c == G and s == 0), stop=(c == 0 and s == 3))
            last.then_inc(av_done, 1)

        @block.tensor
        def _(pe):
            with pe.Fori(0, NP) as hp:
                for step in range(K + LA):
                    if step < K:
                        scores(pe, hp, step)
                    if 0 <= step - LT < K:
                        transposes(pe, hp, step - LT)
                    if 0 <= step - LA < K:
                        values(pe, hp, step - LA)

        @block.scalar
        def _(act):
            for s in stored:
                act.sem_inc(s, 16)
            with act.Fori(0, NP) as hp:
                for step in range(K + LA + 2):
                    if step < K:
                        act.wait_ge(z_done, hp * K + step + 1)
                        act.wait_ge(scanned, hp * 2 * K + 2 * step + 2)
                        G, c = units[step // 4]
                        if c == G:
                            for i in range(2):
                                cols = slice(i * GT, i * GT + keys_of(c, G, 2 * (step % 2) + i))
                                done = nc.scalar.activation(stay[:, step % 4, cols], z[step % 2][:, cols], ACT.Sigmoid,
                                                            scale=-scale)
                        else:
                            done = nc.scalar.activation(stay[:, step % 4, :], z[step % 2][:], ACT.Sigmoid, scale=-scale)
                        done.then_inc(stay_ready, 1)
                    t = step - LT
                    if 0 <= t < K:
                        act.wait_ge(rt_done[0], 12 + hp * K + t + 1)
                        act.wait_ge(av_done, hp * K + t + 1)
                        queries = slice(query_start(units[t // 4][1], units[t // 4][0], t % 4), GT)
                        nc.scalar.activation(RT[:, 0, t % 4, queries], rt[0][:, queries], ACT.Copy).then_inc(rt_copied[0], 1)
                    v = step - LA - 1
                    if v >= 0 and v % 4 == 3 and units[v // 4][1] == 0:
                        G = units[v // 4][0]
                        act.wait_ge(av_done, 4 + hp * K + v + 1)
                        act.wait_ge(stored[G % 2], hp * 16 * (NG // 2) + 16 * (G // 2) + 16)
                        for qt in range(TT):
                            cols = slice(qt * P, (qt + 1) * P)
                            done = nc.scalar.activation(stage[:, G % 2, cols], out[G % 2][:, cols], ACT.Identity,
                                                        bias=k.v_last[:, bass.ds(hp * NT + G * TT + qt, 1)])
                        done.then_inc(out_copied, 1)
                        act.wait_ge(out_copied, 2 + hp * NG + G + 1)
                        act.dma_start(io.mix_t[bass.ds(hp * P, P), G * GT:(G + 1) * GT],
                                      stage[:, G % 2, :]).then_inc(stored[G % 2], 16)
            for s in stored:
                act.wait_ge(s, 16 * (NP * NG // 2 + 1))

        @block.vector
        def _(dve):
            dve.sem_inc(stay_ready, 2)
            dve.sem_inc(scanned, 8)
            dve.sem_inc(av_done, 4)
            dve.sem_inc(out_copied, 2)
            for h in range(2):
                dve.sem_inc(rt_done[h], 12)
                dve.sem_inc(rt_copied[h], 1)
            with dve.Fori(0, NP) as hp:
                for step in range(K + LT):
                    t = step - LT
                    if 0 <= t < K:
                        dve.wait_ge(rt_done[1], 12 + hp * K + t + 1)
                        dve.wait_ge(av_done, hp * K + t + 1)
                        queries = slice(query_start(units[t // 4][1], units[t // 4][0], t % 4), GT)
                        nc.vector.tensor_copy(RT[:, 1, t % 4, queries], rt[1][:, queries]).then_inc(rt_copied[1], 1)
                    if step < K:
                        n, s = divmod(step, 4)
                        G, c = units[n]
                        h = s // 2
                        dve.wait_ge(stay_ready, 2 + hp * K + step + 1)
                        dve.wait_ge(rt_done[h], hp * K + 4 * n + 4)
                        for i in range(2):
                            qt = 2 * (s % 2) + i
                            if c == G:
                                initial = 1.0
                            else:
                                dve.wait_ge(scanned, 8 + hp * 8 * U + 8 * (n - 1) + 4 * h + qt + 1)
                                initial = R[:, (n - 1) % 3, h, qt, 0:1]
                            width = keys_of(c, G, qt)
                            src = stay[:, step % 4, i * GT:i * GT + width]
                            nc.vector.tensor_tensor_scan(R[:, n % 3, h, qt, 0:width][:, ::-1], src[:, ::-1], src[:, ::-1],
                                                         initial, ALU.mult, ALU.bypass).then_inc(scanned, 1)


def mix(nc, k, io):
    with ExitStack() as outer:
        sb, ps, sem = alloc(nc, outer)
        weights = SplitWeights(nc, io.w_out, D, sb, sem, "mix_", gain=k.g_mix)
        with ExitStack() as ctx:
            sb, ps, sem = alloc(nc, ctx)
            RING = 4
            NR = NGRP + NE
            w_router = sb("mix_w_router", [P, DC, NR])
            g_norm2 = sb("mix_g_norm2", [P, D])
            raw = sb("mix_raw", [P, RING, DC, P])
            hi = sb("mix_hi", [P, RING, DC, P], F32R)
            lo = sb("mix_lo", [P, RING, DC, P], F32R)
            sq = sb("mix_sq", [P, 2, DC, P])
            sq2 = sb("mix_sq2", [P, 2, DC // 2, P])
            x = sb("mix_x", [P, RING, D])
            h = sb("mix_h", [P, RING, D])
            u2 = sb("mix_u2", [P, RING, D])
            u2_t = sb("mix_u2_t", [P, 2, DC, P])
            junk = sb("mix_junk", [P, D])
            rms, rinv = sb("mix_rms", [P, 2]), sb("mix_rinv", [P, 2])
            sum2, rms2, rinv2 = sb("mix_sum2", [P, 1]), sb("mix_rms2", [P, 1]), sb("mix_rinv2", [P, 1])
            half_out = [[ps(f"mix_out{half}{n}", [P, GT]) for n in range(2)] for half in range(2)]
            sums = ps("mix_sums", [P, 2])
            tr = [ps(f"mix_tr{i}", [P, GT]) for i in range(2)]
            logits = ps("mix_logits", [P, NR])
            params = sem("mix_params")
            raw_loaded = [sem(f"mix_raw_loaded{i}") for i in range(RING)]
            x_loaded = [sem(f"mix_x_loaded{i}") for i in range(RING)]
            hi_ready = sem("mix_hi_ready")
            sq_ready = sem("mix_sq_ready")
            lo_ready = sem("mix_lo_ready")
            sq2_ready = sem("mix_sq2_ready")
            sums_done = sem("mix_sums_done")
            rms_ready = sem("mix_rms_ready")
            rinv_ready = sem("mix_rinv_ready")
            first_done = sem("mix_first_done")
            second_done = sem("mix_second_done")
            half_ready = sem("mix_half_ready")
            h_ready = sem("mix_h_ready")
            squared = sem("mix_squared")
            rms2_ready = sem("mix_rms2_ready")
            rinv2_ready = sem("mix_rinv2_ready")
            u2_ready = sem("mix_u2_ready")
            u2_transposed = sem("mix_u2_transposed")
            u2_t_ready = sem("mix_u2_t_ready")
            logits_done = sem("mix_logits_done")
            logits_ready = sem("mix_logits_ready")
            stored = [sem(f"mix_stored{i}") for i in range(RING)]
            block = ctx.enter_context(nc.Block())

            def groups(engine, group):
                group(engine, 0, True, False)
                with engine.Fori(1, NG - 1) as G:
                    group(engine, G, False, False)
                group(engine, NG - 1, False, True)

            def load(sp, G, t):
                T = G * RING + t
                sp.dma_start(raw[:, t, :, :], io.mix_t[:, bass.ds(T * P, P)].rearrange("(c p) s -> p c s", p=P)
                             ).then_inc(raw_loaded[t], 16)
                sp.dma_start(x[:, t, :], io.x[bass.ds(T * P, P), :]).then_inc(x_loaded[t], 16)

            def sp_group(sp, G, first, last):
                for t in range(RING):
                    T = G * RING + t
                    hold(sp, k, h_ready, T * 2 + 4)
                    if not last:
                        load(sp, G + 1, t)
                    hold(sp, k, u2_ready, T + 2)
                    sp.dma_start(io.h[bass.ds(T * P, P), :], h[:, t, :]).then_inc(stored[t], 16)
                    sp.dma_start(io.u2[bass.ds(T * P, P), :], u2[:, t, :]).then_inc(stored[t], 16)

            @block.sync
            def _(sp):
                for s in stored:
                    sp.sem_inc(s, 32)
                sp.dma_start(g_norm2[:], io.norm2_g.unsqueeze(0).partition_broadcast(P)).then_inc(params, 16)
                with nc.allow_non_contiguous_dma(reason="router weights, once"):
                    sp.dma_start(w_router[:, :, 0:NGRP], io.w_group.rearrange("(c p) n -> p c n", p=P)).then_inc(params, 16)
                    sp.dma_start(w_router[:, :, NGRP:], io.w_fine.rearrange("(c p) n -> p c n", p=P)).then_inc(params, 16)
                load(sp, 0, 0)
                weights.load(sp)
                for t in range(1, RING):
                    load(sp, 0, t)
                groups(sp, sp_group)
                for s in stored:
                    sp.wait_ge(s, 32 * (NG + 1))

            def pool_group(pool, G, first, last):
                for t in range(RING):
                    T = G * RING + t
                    pool.wait_ge(sq_ready, T + 1)
                    pool.wait_ge(sums_done, T + 1)
                    pairs = sq[:, t % 2, :, :].rearrange("p (c two) s -> p c two s", two=2)
                    nc.gpsimd.tensor_tensor(sq2[:, t % 2, :, :], pairs[:, :, 0, :], pairs[:, :, 1, :], ALU.add).then_inc(sq2_ready, 1)

            @block.gpsimd
            def _(pool):
                groups(pool, pool_group)

            def pe_transposes(pe, T, t):
                pe.wait_ge(u2_ready, T + 2)
                pe.wait_ge(u2_t_ready, T + 1)
                for c in range(DC):
                    last = nc.tensor.transpose(tr[c // 4][:, (c % 4) * P:(c % 4 + 1) * P], u2[:, t, c * P:(c + 1) * P],
                                               k.ident[:])
                last.then_inc(u2_transposed, 1)

            def pe_logits(pe, T, t):
                pe.wait_ge(u2_t_ready, T + 2)
                pe.wait_ge(logits_ready, T + 1)
                for c in range(DC):
                    last = nc.tensor.matmul(logits[:], u2_t[:, t % 2, c, :], w_router[:, c, :],
                                            start=(c == 0), stop=(c == DC - 1))
                last.then_inc(logits_done, 1)

            def pe_group(pe, G, first, last):
                for t in range(RING):
                    T = G * RING + t
                    before = not (first and t == 0)
                    pe.wait_ge(sq2_ready, T + 3)
                    pe.wait_ge(rms_ready, T + 1)
                    for half in range(2):
                        for c in range(NP // 2):
                            end = nc.tensor.matmul(sums[:, half:half + 1], sq2[:, t % 2, half * NP // 2 + c, :], k.ones[:],
                                                   start=(c == 0), stop=(c == NP // 2 - 1))
                    end.then_inc(sums_done, 1)
                    pe.wait_ge(lo_ready, T + 1)
                    for half in range(2):
                        for n in range(2):
                            pe.wait_ge((half_ready, h_ready)[half], T * 2 + n + 1)
                            for c in range(half * NP, half * NP + NP):
                                for m, (a, w) in enumerate(((hi, weights.hi), (lo, weights.hi), (hi, weights.lo))):
                                    end = nc.tensor.matmul(half_out[half][n][:], a[:, t, c, :],
                                                           w[:, c, n * GT:(n + 1) * GT],
                                                           start=(c == half * NP and m == 0),
                                                           stop=(c == half * NP + NP - 1 and m == 2))
                            end.then_inc((first_done, second_done)[half], 1)
                        if half == 0 and before:
                            pe_transposes(pe, T - 1, (t - 1) % RING)
                    if before:
                        pe_logits(pe, T - 1, (t - 1) % RING)

            @block.tensor
            def _(pe):
                pe.wait_ge(params, 48)
                pe.wait_ge(weights.low_ready, DC)
                groups(pe, pe_group)
                pe_transposes(pe, NT - 1, RING - 1)
                pe_logits(pe, NT - 1, RING - 1)

            def act_inputs(act, G, t):
                T = G * RING + t
                act.wait_ge(raw_loaded[t], G * 16 + 16)
                act.wait_ge(second_done, T * 2 + 2)
                nc.scalar.activation(hi[:, t, :, :], raw[:, t, :, :], ACT.Copy).then_inc(hi_ready, 1)
                act.wait_ge(sq2_ready, T + 1)
                nc.scalar.activation(sq[:, t % 2, :, :], raw[:, t, :, :], ACT.Square).then_inc(sq_ready, 1)

            def act_u2_t(act, T, t):
                act.wait_ge(u2_transposed, T + 1)
                act.wait_ge(logits_done, T + 1)
                for i in range(2):
                    end = nc.scalar.activation(u2_t[:, t % 2, 4 * i:4 * i + 4, :], tr[i][:].rearrange("p (c n) -> p c n", c=4), ACT.Copy)
                end.then_inc(u2_t_ready, 1)

            def act_group(act, G, first, last):
                for t in range(RING):
                    T = G * RING + t
                    act.wait_ge(sums_done, T + 3)
                    act.wait_ge(rinv_ready, T + 1)
                    nc.scalar.activation(rms[:], sums[:], ACT.Sqrt, scale=1.0 / W_SB, bias=k.eps[:]).then_inc(rms_ready, 1)
                    if t < RING - 1:
                        act_inputs(act, G, t + 1)
                    elif not last:
                        act_inputs(act, G + 1, 0)
                    if not (first and t == 0):
                        act_u2_t(act, T - 1, (t - 1) % RING)
                    act.wait_ge(h_ready, T * 2 + 4)
                    act.wait_ge(rms2_ready, T + 1)
                    act.wait_ge(squared, T + 1)
                    nc.scalar.activation(junk[:], h[:, t, :], ACT.Square, accum_out=sum2[:]).then_inc(squared, 1)
                    act.wait_ge(squared, T + 2)
                    act.wait_ge(rinv2_ready, T + 1)
                    nc.scalar.activation(rms2[:], sum2[:], ACT.Sqrt, scale=1.0 / D, bias=k.eps[:]).then_inc(rms2_ready, 1)

            @block.scalar
            def _(act):
                act_inputs(act, 0, 0)
                weights.high(act)
                groups(act, act_group)
                act_u2_t(act, NT - 1, RING - 1)

            def dve_low(dve, G, t):
                T = G * RING + t
                dve.wait_ge(hi_ready, T + 1)
                nc.vector.tensor_tensor(lo[:, t, :, :], raw[:, t, :, :], f32(hi[:, t, :, :]), ALU.subtract).then_inc(lo_ready, 1)

            def dve_logits(dve, T):
                dve.wait_ge(logits_done, T + 3)
                nc.vector.tensor_tensor(k.logits[:, bass.ds(T * NR, NR)], logits[:], k.b_router[:], ALU.add).then_inc(logits_ready, 1)

            def dve_group(dve, G, first, last):
                for t in range(RING):
                    T = G * RING + t
                    dve.wait_ge(rms_ready, T + 2)
                    dve.wait_ge(h_ready, T * 2 + 2)
                    nc.vector.reciprocal(rinv[:], rms[:]).then_inc(rinv_ready, 1)
                    dve.wait_ge(rinv_ready, T + 2)
                    dve.wait_ge(x_loaded[t], G * 16 + 16)
                    dve.wait_ge(stored[t], G * 32 + 32)
                    for n in range(2):
                        cols = slice(n * GT, (n + 1) * GT)
                        dve.wait_ge(first_done, T * 2 + n + 1)
                        nc.vector.scalar_tensor_tensor(h[:, t, cols], half_out[0][n][:], rinv[:, 0:1], x[:, t, cols],
                                                       ALU.mult, ALU.add).then_inc(half_ready, 1)
                    if t < RING - 1:
                        dve_low(dve, G, t + 1)
                    elif not last:
                        dve_low(dve, G + 1, 0)
                    for n in range(2):
                        cols = slice(n * GT, (n + 1) * GT)
                        dve.wait_ge(second_done, T * 2 + n + 1 + 2 * RING)
                        dve.wait_ge(half_ready, T * 2 + n + 3)
                        nc.vector.scalar_tensor_tensor(h[:, t, cols], half_out[1][n][:], rinv[:, 1:2], h[:, t, cols],
                                                       ALU.mult, ALU.add).then_inc(h_ready, 1)
                    if not (first and t == 0):
                        dve_logits(dve, T - 1)
                    dve.wait_ge(rms2_ready, T + 2)
                    dve.wait_ge(u2_ready, T + 1)
                    nc.vector.reciprocal(rinv2[:], rms2[:]).then_inc(rinv2_ready, 1)
                    dve.wait_ge(rinv2_ready, T + 2)
                    nc.vector.scalar_tensor_tensor(u2[:, t, :], h[:, t, :], rinv2[:], g_norm2[:],
                                                   ALU.mult, ALU.mult).then_inc(u2_ready, 1)

            @block.vector
            def _(dve):
                for s, start in ((sums_done, 2), (sq2_ready, 2), (rms_ready, 1), (rinv_ready, 1), (second_done, 2 * RING),
                                 (half_ready, 2), (h_ready, 2), (squared, 1), (rms2_ready, 1), (rinv2_ready, 1),
                                 (u2_ready, 1), (u2_t_ready, 1), (logits_done, 2), (logits_ready, 1)):
                    dve.sem_inc(s, start)
                dve.wait_ge(params, 48)
                dve_low(dve, 0, 0)
                weights.low(dve)
                groups(dve, dve_group)
                dve_logits(dve, NT - 1)


class ExpertWeights:

    def __init__(self, nc, k, io, sb, sem):
        self.nc, self.k = nc, k
        self.src = [io.w_e_gate, io.w_e_up, io.w_e_down]
        self.chunks = [DC, DC, FC]
        self.raw = sb("ew_raw", [P, MATRICES, WM])
        self.hi = sb("ew_hi", [P, MATRICES, WM], F32R)
        self.lo = sb("ew_lo", [P, MATRICES, WM], F32R)
        self.loaded = [sem(f"ew_loaded{m}") for m in range(MATRICES)]
        self.high_ready = [sem(f"ew_high_ready{m}") for m in range(MATRICES)]
        self.low_ready = [sem(f"ew_low_ready{m}") for m in range(MATRICES)]

    def load(self, sp, e):
        for m in range(MATRICES):
            if not isinstance(e, int):
                hold(sp, self.k, self.low_ready[m], e * PIECES)
            elif e > 0:
                sp.wait_ge(self.low_ready[m], e * PIECES)
            one = self.src[m][bass.ds(e, 1)].rearrange("e (c p) n -> p (e c) n", p=P)
            sp.dma_start(self.raw[:, m, :].rearrange("p (c n) -> p c n", c=self.chunks[m]), one).then_inc(self.loaded[m], 16)

    def high(self, act, m, e):
        act.wait_ge(self.loaded[m], e * 16 + 16)
        for i in range(PIECES):
            cols = slice(i * WM // PIECES, (i + 1) * WM // PIECES)
            self.nc.scalar.activation(self.hi[:, m, cols], self.raw[:, m, cols], ACT.Copy).then_inc(self.high_ready[m], 1)

    def low(self, engine, m, e, pieces=range(PIECES)):
        for i in pieces:
            cols = slice(i * WM // PIECES, (i + 1) * WM // PIECES)
            engine.wait_ge(self.high_ready[m], e * PIECES + i + 1)
            engine.tensor_tensor(self.lo[:, m, cols], self.raw[:, m, cols], f32(self.hi[:, m, cols]),
                                 ALU.subtract).then_inc(self.low_ready[m], 1)

    def passes(self, a_hi, a_lo, m, chunks, col):
        row = WM // self.chunks[m]
        for a, w in ((a_hi, self.hi), (a_hi, self.lo), (a_lo, self.hi)):
            for c in chunks:
                yield a, a[:, c, :], w[:, m, c * row + col:c * row + col + GT]


def route(nc, k, io):
    with ExitStack() as ctx:
        sb, ps, sem = alloc(nc, ctx)
        NR = NGRP + NE
        iota_i = sb("rt_iota_i", [P, P], I32)
        iota = sb("rt_iota", [P, P])
        token_i, token_f = sb("rt_token_i", [P, NT], I32), sb("rt_token_f", [P, NT])
        small = lambda name, *shape: sb("rt_" + name, [P, NT, *shape])
        g_max, g_dist, g_exp, g_sum, g_prob = small("g_max"), small("g_dist", NGRP), small("g_exp", NGRP), small("g_sum"), small("g_prob")
        g_eq, g_cand, g_first, g_hot, g_pen = small("g_eq", NGRP), small("g_cand", NGRP), small("g_first"), small("g_hot", NGRP), small("g_pen", NGRP)
        fines = sb("rt_fines", [P, TOPK, NT * NE])
        fine = [fines[:, i, :].rearrange("p (t e) -> p t e", e=NE) for i in range(TOPK)]
        top, first = [small(f"top{i}") for i in range(TOPK)], [small(f"first{i}") for i in range(TOPK)]
        hots = sb("rt_hots", [P, TOPK, NT * NE])
        hot = [hots[:, i, :].rearrange("p (t e) -> p t e", e=NE) for i in range(TOPK)]
        eq, cand = small("eq", NE), small("cand", NE)
        dist, ratio, denom, share = small("dist"), small("ratio"), small("denom"), small("share")
        both = sb("rt_both", [P, NT * NE], BF16)
        seg = sb("rt_seg", [P, NE, NT])
        sums = sb("rt_sums", [P, 2, NE * NT])
        totals, upto = (sums[:, i, :].rearrange("p (e t) -> p e t", t=NT) for i in range(2))
        base = sb("rt_base", [P, NE, NT])
        slot_all, picked = eq, cand
        slot_f = small("slot_f")
        count_f, tiles_f, end_f, start_f, ones_e = (sb("rt_" + n, [P, NE]) for n in ("count_f", "tiles_f", "end_f", "start_f", "ones_e"))
        count_i = sb("rt_count_i", [P, NE], I32)
        tiles_i = sb("rt_tiles_i", [P, NE], I32)
        lane_i, row_i = (sb("rt_" + n, [P, NT], I32) for n in ("lane_i", "row_i"))
        lane_f, row_f = (sb("rt_" + n, [P, TOPK, NT]) for n in ("lane_f", "row_f"))
        BT = 8
        lane_hot = fines[:].rearrange("p b (t n) -> p b t n", t=BT)
        row_hot = hots[:, :, 0:BT * WIDE].rearrange("p b (t n) -> p b t n", t=BT)
        below = sums[0:1, :, :].rearrange("p i n -> p (i n)").bitcast(BF16)[:, 0:WIDE * NE].rearrange("p (t e) -> p t e", e=NE)
        expert_f = sb("rt_expert_f", [1, WIDE])
        pairs_i, pairs_f = sb("rt_pairs_i", [1, 1], I32), sb("rt_pairs_f", [1, 1])
        prefix = [ps(f"rt_prefix{i}", [P, GT]) for i in range(2)]
        total = [ps(f"rt_total{i}", [P, GT]) for i in range(2)]
        place = ps("rt_place", [P, WIDE])
        placed, hot_ready = sem("rt_placed"), sem("rt_hot_ready")
        iota_ready, step, g_exp_ready, ratio_ready = sem("rt_iota_ready"), sem("rt_step"), sem("rt_g_exp_ready"), sem("rt_ratio_ready")
        counted = sem("rt_counted")
        g_dist_ready, dist_ready, both_ready = sem("rt_g_dist_ready"), sem("rt_dist_ready"), sem("rt_both_ready")
        logits = k.logits[:].rearrange("p (t n) -> p t n", n=NR)
        weights = k.weights
        block = ctx.enter_context(nc.Block())

        def spread(ap, n):
            return ap.unsqueeze(2).to_broadcast([P, NT, n])

        def along(n):
            return iota[:, 0:n].unsqueeze(1).to_broadcast([P, NT, n])

        @block.gpsimd
        def _(pool):
            nc.gpsimd.iota(iota_i[:], pattern=[[1, P]], base=0, channel_multiplier=0)
            nc.gpsimd.iota(token_i[:], pattern=[[P, NT]], base=0, channel_multiplier=1)
            nc.gpsimd.memset(ones_e[:], 1.0)
            nc.gpsimd.memset(seg[:], 1.0).then_inc(iota_ready, 1)
            pool.wait_ge(iota_ready, 1)
            nc.gpsimd.memset(seg[:, :, 0:1], 0.0).then_inc(iota_ready, 1)
            for m in range(MATRICES):
                weights.low(pool, m, 0)

        @block.sync
        def _(sp):
            for e in range(2):
                weights.load(sp, e)

        @block.scalar
        def _(act):
            act.wait_ge(g_dist_ready, 1)
            nc.scalar.activation(g_exp[:], g_dist[:], ACT.Exp).then_inc(g_exp_ready, 1)
            act.wait_ge(dist_ready, 1)
            nc.scalar.activation(ratio[:], dist[:], ACT.Exp).then_inc(ratio_ready, 1)
            for m in range(MATRICES):
                weights.high(act, m, 0)

        @block.tensor
        def _(pe):
            pe.wait_ge(both_ready, 1)
            for i in range(2):
                nc.tensor.matmul(prefix[i][:], k.before[:], both[:, i * GT:(i + 1) * GT], start=True, stop=True)
            for i in range(2):
                last = nc.tensor.matmul(total[i][:], k.ones_bf[:], both[:, i * GT:(i + 1) * GT], start=True, stop=True)
            last.then_inc(counted, 1)
            for turn in range(TOPK * NT // BT):
                pe.wait_ge(hot_ready, turn + 1)
                for t in range(BT):
                    last = nc.tensor.matmul(place[:], lane_hot[:, turn % 2, t, :], row_hot[:, turn % 2, t, :],
                                            start=(turn == 0 and t == 0), stop=(turn == TOPK * NT // BT - 1 and t == BT - 1))
                last.then_inc(placed, 1)

        @block.vector
        def _(dve):
            count = [0]

            def link(instruction):
                count[0] += 1
                instruction.then_inc(step, 1)
                dve.wait_ge(step, count[0])

            def done(sem_ready):
                dve.sem_inc(sem_ready, 1)

            V = nc.vector
            dve.wait_ge(iota_ready, 2)
            link(V.tensor_copy(iota[:], iota_i[:]))
            link(V.tensor_copy(token_f[:], token_i[:]))
            g_logits = logits[:, :, 0:NGRP]
            link(V.tensor_reduce(g_max[:], g_logits, AX.X, ALU.max))
            link(V.tensor_tensor(g_dist[:], g_logits, spread(g_max[:], NGRP), ALU.subtract))
            done(g_dist_ready)
            link(V.tensor_scalar(g_eq[:], g_dist[:], 0.0, None, ALU.is_equal))
            link(V.scalar_tensor_tensor(g_cand[:], g_eq[:], -2.0 * NE, along(NGRP), ALU.mult, ALU.add))
            link(V.tensor_reduce(g_first[:], g_cand[:], AX.X, ALU.min))
            link(V.tensor_tensor(g_hot[:], g_cand[:], spread(g_first[:], NGRP), ALU.is_equal))
            link(V.tensor_scalar(g_pen[:], g_hot[:], -MASKED, MASKED, ALU.mult, ALU.add))
            link(V.tensor_tensor(fine[0].rearrange("p t (g e) -> p t g e", g=NGRP),
                                 logits[:, :, NGRP:].rearrange("p t (g e) -> p t g e", g=NGRP),
                                 g_pen[:].unsqueeze(3).to_broadcast([P, NT, NGRP, EPG]), ALU.add))
            for c in range(TOPK):
                link(V.tensor_reduce(top[c][:], fine[c], AX.X, ALU.max))
                link(V.tensor_tensor(eq[:], fine[c], spread(top[c][:], NE), ALU.is_equal))
                link(V.scalar_tensor_tensor(cand[:], eq[:], -2.0 * NE, along(NE), ALU.mult, ALU.add))
                link(V.tensor_reduce(first[c][:], cand[:], AX.X, ALU.min))
                link(V.tensor_tensor(hot[c], cand[:], spread(first[c][:], NE), ALU.is_equal))
                if c == 0:
                    link(V.scalar_tensor_tensor(fine[1], hot[0], 3 * MASKED, fine[0], ALU.mult, ALU.add))
            link(V.tensor_tensor(both[:].rearrange("p (t e) -> p t e", e=NE), hot[0], hot[1], ALU.add))
            done(both_ready)
            link(V.tensor_tensor(dist[:], top[1][:], top[0][:], ALU.subtract))
            done(dist_ready)
            dve.wait_ge(g_exp_ready, 1)
            link(V.tensor_reduce(g_sum[:], g_exp[:], AX.X, ALU.add))
            link(V.reciprocal(g_prob[:], g_sum[:]))
            dve.wait_ge(ratio_ready, 1)
            link(V.tensor_scalar(denom[:], ratio[:], 1.0, None, ALU.add))
            link(V.reciprocal(share[:], denom[:]))
            link(V.tensor_tensor(k.weight[:, 0, :], share[:], g_prob[:], ALU.mult))
            link(V.tensor_tensor(k.weight[:, 1, :], k.weight[:, 0, :], ratio[:], ALU.mult))
            dve.wait_ge(counted, 1)
            for i in range(2):
                half = NT // 2
                link(V.tensor_copy(totals[:, :, i * half:(i + 1) * half], total[i][:].rearrange("p (t e) -> p e t", e=NE)))
            flat = lambda ap: ap[:].rearrange("p e t -> p (e t)")
            link(V.tensor_tensor_scan(flat(upto), flat(seg), flat(totals), 0.0, ALU.mult, ALU.add))
            link(V.tensor_tensor(base[:], upto[:], totals[:], ALU.subtract))
            link(V.tensor_scalar(count_f[:], upto[:, :, NT - 1], float(P - 1), None, ALU.add))
            link(V.tensor_copy(count_i[:], count_f[:]))
            link(V.tensor_scalar(tiles_i[:], count_i[:], 7, None, ALU.logical_shift_right))
            link(V.tensor_copy(tiles_f[:], tiles_i[:]))
            link(V.tensor_scalar(tiles_f[:], tiles_f[:], 1.0, None, ALU.max))
            link(V.tensor_tensor_scan(end_f[:], ones_e[:], tiles_f[:], 0.0, ALU.mult, ALU.add))
            link(V.tensor_tensor(start_f[:], end_f[:], tiles_f[:], ALU.subtract))
            link(V.scalar_tensor_tensor(base[:], start_f[:].unsqueeze(2).to_broadcast([P, NE, NT]), float(P), base[:], ALU.mult, ALU.add))
            for i in range(2):
                half = NT // 2
                link(V.tensor_tensor(slot_all[:, i * half:(i + 1) * half, :], prefix[i][:].rearrange("p (t e) -> p t e", e=NE),
                                     base[:, :, i * half:(i + 1) * half].rearrange("p e t -> p t e"), ALU.add))
            for c in range(TOPK):
                link(V.tensor_tensor(picked[:], slot_all[:], hot[c], ALU.mult))
                link(V.tensor_reduce(slot_f[:], picked[:], AX.X, ALU.add))
                link(V.tensor_copy(k.slot[:, c, :], slot_f[:]))
                link(V.tensor_scalar(lane_i[:], k.slot[:, c, :], P - 1, None, ALU.bitwise_and))
                link(V.tensor_scalar(row_i[:], k.slot[:, c, :], 7, None, ALU.logical_shift_right))
                link(V.tensor_copy(lane_f[:, c, :], lane_i[:]))
                link(V.tensor_copy(row_f[:, c, :], row_i[:]))
            for turn in range(TOPK * NT // BT):
                c, t = divmod(turn * BT, NT)
                if turn >= 2:
                    dve.wait_ge(placed, turn - 1)
                wide = lambda ap, n: ap.unsqueeze(2).to_broadcast([P, BT, n])
                all_of = lambda n: iota[:, 0:n].unsqueeze(1).to_broadcast([P, BT, n])
                link(V.tensor_tensor(lane_hot[:, turn % 2, :, :], wide(lane_f[:, c, t:t + BT], P), iota[:].unsqueeze(1).to_broadcast([P, BT, P]), ALU.is_equal))
                link(V.tensor_tensor(row_hot[:, turn % 2, :, :], wide(row_f[:, c, t:t + BT], WIDE), all_of(WIDE), ALU.is_equal))
                link(V.tensor_tensor(row_hot[:, turn % 2, :, :], row_hot[:, turn % 2, :, :], wide(token_f[:, t:t + BT], WIDE), ALU.mult))
                done(hot_ready)
            link(V.tensor_tensor(below, end_f[0:1, :].unsqueeze(1).to_broadcast([1, WIDE, NE]),
                                 iota[0:1, 0:WIDE].unsqueeze(2).to_broadcast([1, WIDE, NE]), ALU.is_le))
            link(V.tensor_reduce(expert_f[:], below, AX.X, ALU.add))
            link(V.tensor_scalar(expert_f[:], expert_f[:], float(NE - 1), None, ALU.min))
            link(V.tensor_copy(k.tile_expert[:], expert_f[:]))
            link(V.tensor_tensor(k.tile_last[0:1, 0:WIDE - 1], expert_f[0:1, 1:WIDE], expert_f[0:1, 0:WIDE - 1], ALU.subtract))
            link(V.tensor_copy(k.tile_count[:], end_f[0:1, NE - 1:NE]))
            dve.wait_ge(placed, TOPK * NT // BT)
            link(V.tensor_copy(k.ids[:], place[:]))


def experts(nc, k, io):
    with ExitStack() as ctx:
        sb, ps, sem = alloc(nc, ctx)
        weights = k.weights
        index = sb("ex_index", [P, 1], I32)
        xg = sb("ex_xg", [P, D])
        x_hi, x_lo = sb("ex_x_hi", [P, DC, P], F32R), sb("ex_x_lo", [P, DC, P], F32R)
        silu = sb("ex_silu", [P, DE])
        hidden = sb("ex_hidden", [P, DE])
        h_hi, h_lo = sb("ex_h_hi", [P, FC, P], F32R), sb("ex_h_lo", [P, FC, P], F32R)
        y = sb("ex_y", [P, D])
        gate, up = ps("ex_gate", [P, DE]), ps("ex_up", [P, DE])
        h_tr = [ps(f"ex_h_tr{i}", [P, GT])[:, 0:2 * P] for i in range(2)]
        x_tr = [ps(f"ex_x_tr{i}", [P, GT]) for i in range(2)]
        down = [ps(f"ex_down{i}", [P, GT]) for i in range(2)]
        index_ready = sem("ex_index_ready")
        gathered = k.x_gathered
        x_transposed = [sem(f"ex_x_transposed{i}") for i in range(2)]
        x_hi_ready = [sem(f"ex_x_hi_ready{i}") for i in range(2)]
        x_lo_ready = [sem(f"ex_x_lo_ready{i}") for i in range(2)]
        gate_done, up_done = sem("ex_gate_done"), sem("ex_up_done")
        silu_ready = sem("ex_silu_ready")
        hidden_ready = [sem(f"ex_hidden_ready{i}") for i in range(2)]
        h_transposed = [sem(f"ex_h_transposed{i}") for i in range(2)]
        h_hi_ready = [sem(f"ex_h_hi_ready{i}") for i in range(2)]
        h_lo_ready = sem("ex_h_lo_ready")
        down_first = sem("ex_down_first")
        tiles_done = sem("ex_tiles_done")
        y_ready = [sem(f"ex_y_ready{i}") for i in range(2)]
        y_stored = sem("ex_y_stored")
        block = ctx.enter_context(nc.Block())

        def tiles(engine):
            return engine.value_load(k.tile_count[0:1, 0:1], min_val=NE, max_val=MAX_TILES)

        def expert(engine, T):
            return engine.value_load(k.tile_expert[0:1, bass.ds(T, 1)], min_val=0, max_val=NE - 1)

        def last_tile(engine, T):
            return engine.to_reg(engine.value_load(k.tile_last[0:1, bass.ds(T, 1)], min_val=0, max_val=1))

        @block.sync
        def _(sp):
            with sp.Fori(2, NE) as e:
                weights.load(sp, e)

        @block.gpsimd
        def _(pool):
            def gather():
                pool.indirect_dma_start(out=xg[:], out_offset=None, in_=io.u2,
                                        in_offset=bass.IndirectOffsetOnAxis(ap=index[:], axis=0)).then_inc(gathered, 16)

            nc.gpsimd.tensor_copy(index[:], k.ids[:, 0:1]).then_inc(index_ready, 1)
            pool.wait_ge(index_ready, 1)
            gather()
            with pool.Fori(0, tiles(pool)) as T:
                pool.wait_ge(x_transposed[1], T + 1)
                nc.gpsimd.tensor_copy(index[:], k.ids[:, bass.ds(T + 1, 1)]).then_inc(index_ready, 1)
                hold(pool, k, index_ready, T + 2)
                gather()

        def transpose_x(pe, half):
            for c in range(4):
                last = nc.tensor.transpose(x_tr[half][:, c * P:(c + 1) * P],
                                           xg[:, (4 * half + c) * P:(4 * half + c + 1) * P], k.ident[:])
            last.then_inc(x_transposed[half], 1)

        @block.tensor
        def _(pe):
            pe.wait_ge(gathered, 16)
            for half in range(2):
                transpose_x(pe, half)
            with pe.Fori(0, tiles(pe)) as T:
                e = expert(pe, T)
                pe.wait_ge(hidden_ready[1], T + 1)
                for m, dst, done in ((0, gate, gate_done), (1, up, up_done)):
                    pe.wait_ge(weights.low_ready[m], e * PIECES + PIECES)
                    for n, (a, x, w) in enumerate(weights.passes(x_hi, x_lo, m, range(DC), 0)):
                        if m == 0 and n % 4 == 0:
                            ready = x_lo_ready if a is x_lo else x_hi_ready
                            pe.wait_ge(ready[n // 4 % 2], T + 1)
                        last = nc.tensor.matmul(dst[:], x, w, start=(n == 0), stop=(n == 3 * DC - 1))
                    last.then_inc(done, 1)
                pe.wait_ge(gathered, T * 16 + 32)
                for half in range(2):
                    transpose_x(pe, half)
                for half in range(2):
                    pe.wait_ge(hidden_ready[half], T + 2)
                    for f in range(2 * half, 2 * half + 2):
                        last = nc.tensor.transpose(h_tr[half][:, (f % 2) * P:(f % 2 + 1) * P], hidden[:, f * P:(f + 1) * P],
                                                   k.ident[:])
                    last.then_inc(h_transposed[half], 1)
                pe.wait_ge(weights.low_ready[2], e * PIECES + PIECES)
                for n in range(2):
                    pe.wait_ge(y_ready[n], T + 1)
                    for i, (a, h, w) in enumerate(weights.passes(h_hi, h_lo, 2, range(FC), n * GT)):
                        if n == 0 and i in (0, 2):
                            pe.wait_ge(h_hi_ready[i // 2], T + 1)
                        if n == 0 and i == 2 * FC:
                            pe.wait_ge(h_lo_ready, T * 2 + 2)
                        last = nc.tensor.matmul(down[n][:], h, w, start=(i == 0), stop=(i == 3 * FC - 1))
                    last.then_inc((down_first, tiles_done)[n], 1)

        def x_high(act, T, half):
            nc.scalar.activation(x_hi[:, 4 * half:4 * half + 4, :], x_tr[half][:].rearrange("p (c n) -> p c n", c=4),
                                 ACT.Copy).then_inc(x_hi_ready[half], 1)

        def x_low(dve, half):
            chunks = slice(4 * half, 4 * half + 4)
            nc.vector.tensor_tensor(x_lo[:, chunks, :], x_tr[half][:].rearrange("p (c n) -> p c n", c=4),
                                    f32(x_hi[:, chunks, :]), ALU.subtract).then_inc(x_lo_ready[half], 1)

        @block.scalar
        def _(act):
            act.sem_inc(y_stored, 16)
            for half in range(2):
                act.wait_ge(x_transposed[half], 1)
                x_high(act, 0, half)
            with act.Fori(0, tiles(act)) as T:
                e = expert(act, T)
                last = last_tile(act, T)
                act.wait_ge(gate_done, T + 1)
                act.wait_ge(hidden_ready[1], T + 1)
                nc.scalar.activation(silu[:], gate[:], ACT.Silu).then_inc(silu_ready, 1)
                with act.If_eq(last, 1):
                    weights.high(act, 0, e + 1)
                act.wait_ge(tiles_done, T + 1)
                for half in range(2):
                    act.wait_ge(h_transposed[half], T + 2)
                    nc.scalar.activation(h_hi[:, 2 * half:2 * half + 2, :], h_tr[half].rearrange("p (f n) -> p f n", f=2),
                                         ACT.Copy).then_inc(h_hi_ready[half], 1)
                for half in range(2):
                    act.wait_ge(x_transposed[half], T + 2)
                    act.wait_ge(up_done, T + 1)
                    x_high(act, T, half)
                with act.If_eq(last, 1):
                    weights.high(act, 1, e + 1)
                act.wait_ge(down_first, T + 1)
                act.wait_ge(y_stored, T * 16 + 16)
                nc.scalar.activation(y[:, 0:GT], down[0][:], ACT.Copy).then_inc(y_ready[0], 1)
                for half in range(2):
                    act.wait_ge(y_ready[half], T + 2)
                act.dma_start(io.ys[bass.ds(T * P, P), :], y[:]).then_inc(y_stored, 16)
                with act.If_eq(last, 1):
                    weights.high(act, 2, e + 1)
            n = tiles(act)
            hold(act, k, y_stored, n * 16 + 16)

        @block.vector
        def _(dve):
            dve.sem_inc(tiles_done, 1)
            for half in range(2):
                dve.sem_inc(hidden_ready[half], 1)
                dve.sem_inc(h_transposed[half], 1)
                dve.sem_inc(y_ready[half], 1)
            for half in range(2):
                dve.wait_ge(x_hi_ready[half], 1)
                x_low(dve, half)
            with dve.Fori(0, tiles(dve)) as T:
                e = expert(dve, T)
                last = last_tile(dve, T)
                with dve.If_eq(last, 1):
                    weights.low(dve, 0, e + 1, range(PIECES - 1))
                dve.wait_ge(silu_ready, T + 1)
                dve.wait_ge(up_done, T + 1)
                for half in range(2):
                    cols = slice(half * DE // 2, (half + 1) * DE // 2)
                    dve.wait_ge(h_transposed[half], T + 1)
                    nc.vector.tensor_tensor(hidden[:, cols], silu[:, cols], up[:, cols], ALU.mult).then_inc(hidden_ready[half], 1)
                for half in range(2):
                    dve.wait_ge(h_hi_ready[half], T + 1)
                    nc.vector.tensor_tensor(h_lo[:, 2 * half:2 * half + 2, :], h_tr[half].rearrange("p (f n) -> p f n", f=2),
                                            f32(h_hi[:, 2 * half:2 * half + 2, :]), ALU.subtract).then_inc(h_lo_ready, 1)
                with dve.If_eq(last, 1):
                    weights.low(dve, 0, e + 1, [PIECES - 1])
                for half in range(2):
                    dve.wait_ge(x_hi_ready[half], T + 2)
                    x_low(dve, half)
                with dve.If_eq(last, 1):
                    weights.low(dve, 1, e + 1)
                dve.wait_ge(tiles_done, T + 2)
                dve.wait_ge(y_stored, T * 16 + 16)
                nc.vector.tensor_copy(y[:, GT:D], down[1][:]).then_inc(y_ready[1], 1)
                with dve.If_eq(last, 1):
                    weights.low(dve, 2, e + 1)


def routed_experts(nc, k, io):
    with ExitStack() as ctx:
        sb, ps, sem = alloc(nc, ctx)
        k.weights = ExpertWeights(nc, k, io, sb, sem)
        route(nc, k, io)
        experts(nc, k, io)


def combine(nc, k, io):
    with ExitStack() as ctx:
        sb, ps, sem = alloc(nc, ctx)
        RING = 4
        g_final = sb("co_g_final", [P, D])
        index = sb("co_index", [P, RING, TOPK], I32)
        h = sb("co_h", [P, RING, D])
        ye = sb("co_ye", [P, RING, TOPK, D])
        acc = sb("co_acc", [P, RING, D])
        out = sb("co_out", [P, RING, D])
        junk = sb("co_junk", [P, D])
        total, rms, rinv = sb("co_total", [P, 1]), sb("co_rms", [P, 1]), sb("co_rinv", [P, 1])
        params = sem("co_params")
        h_loaded = [sem(f"co_h_loaded{i}") for i in range(RING)]
        gathered = k.y_gathered
        index_ready, acc_ready = sem("co_index_ready"), sem("co_acc_ready")
        sum_ready = sem("co_sum_ready")
        rms_ready, rinv_ready, out_ready = sem("co_rms_ready"), sem("co_rinv_ready"), sem("co_out_ready")
        squared = sem("co_squared")
        stored = [sem(f"co_stored{i}") for i in range(RING)]
        block = ctx.enter_context(nc.Block())

        def groups(engine, group):
            group(engine, 0, True, False)
            with engine.Fori(1, NG - 1) as G:
                group(engine, G, False, False)
            group(engine, NG - 1, False, True)

        def load(sp, G, t):
            sp.dma_start(h[:, t, :], io.h[bass.ds(G * GT + t * P, P), :]).then_inc(h_loaded[t], 16)

        def sp_group(sp, G, first, last):
            for t in range(RING):
                T = G * RING + t
                hold(sp, k, sum_ready, T * 2 + 2)
                if not last:
                    load(sp, G + 1, t)
                hold(sp, k, out_ready, T + 2)
                sp.dma_start(io.out[bass.ds(T * P, P), :], out[:, t, :]).then_inc(stored[t], 16)

        @block.sync
        def _(sp):
            for s in stored:
                sp.sem_inc(s, 16)
            sp.dma_start(g_final[:], io.final_g.unsqueeze(0).partition_broadcast(P)).then_inc(params, 16)
            for t in range(RING):
                load(sp, 0, t)
            groups(sp, sp_group)
            for s in stored:
                sp.wait_ge(s, 16 * (NG + 1))

        def pool_group(pool, G, first, last):
            for t in range(RING):
                T = G * RING + t
                if not first:
                    pool.wait_ge(sum_ready, T * 2 + 2 - 2 * RING)
                for c in range(TOPK):
                    nc.gpsimd.tensor_copy(index[:, t, c:c + 1], k.slot[:, c, bass.ds(T, 1)]).then_inc(index_ready, 1)
                hold(pool, k, index_ready, T * 2 + 2)
                for c in range(TOPK):
                    pool.indirect_dma_start(out=ye[:, t, c, :], out_offset=None, in_=io.ys,
                                            in_offset=bass.IndirectOffsetOnAxis(ap=index[:, t, c:c + 1], axis=0)).then_inc(gathered[t], 16)

        @block.gpsimd
        def _(pool):
            groups(pool, pool_group)

        def act_group(act, G, first, last):
            for t in range(RING):
                T = G * RING + t
                act.wait_ge(sum_ready, T * 2 + 2)
                act.wait_ge(rms_ready, T + 1)
                act.wait_ge(squared, T + 1)
                nc.scalar.activation(junk[:], acc[:, t, :], ACT.Square, accum_out=total[:]).then_inc(squared, 1)
                act.wait_ge(squared, T + 2)
                act.wait_ge(rinv_ready, T + 1)
                nc.scalar.activation(rms[:], total[:], ACT.Sqrt, scale=1.0 / D, bias=k.eps[:]).then_inc(rms_ready, 1)

        @block.scalar
        def _(act):
            groups(act, act_group)

        def dve_group(dve, G, first, last):
            for t in range(RING):
                T = G * RING + t
                dve.wait_ge(h_loaded[t], G * 16 + 16)
                dve.wait_ge(gathered[t], G * 32 + 32)
                dve.wait_ge(out_ready, T + 1)
                nc.vector.scalar_tensor_tensor(acc[:, t, :], ye[:, t, 0, :], k.weight[:, 0, bass.ds(T, 1)], h[:, t, :],
                                               ALU.mult, ALU.add).then_inc(sum_ready, 1)
                dve.wait_ge(sum_ready, T * 2 + 1)
                nc.vector.scalar_tensor_tensor(acc[:, t, :], ye[:, t, 1, :], k.weight[:, 1, bass.ds(T, 1)], acc[:, t, :],
                                               ALU.mult, ALU.add).then_inc(sum_ready, 1)
                dve.wait_ge(rms_ready, T + 2)
                nc.vector.reciprocal(rinv[:], rms[:]).then_inc(rinv_ready, 1)
                dve.wait_ge(rinv_ready, T + 2)
                dve.wait_ge(stored[t], G * 16 + 16)
                nc.vector.scalar_tensor_tensor(out[:, t, :], acc[:, t, :], rinv[:], g_final[:],
                                               ALU.mult, ALU.mult).then_inc(out_ready, 1)

        @block.vector
        def _(dve):
            for s in (squared, rms_ready, rinv_ready, out_ready):
                dve.sem_inc(s, 1)
            dve.wait_ge(params, 16)
            groups(dve, dve_group)


class Names:
    pass


def build(nc, io):
    scratch = lambda name, shape, dt=F32: nc.dram_tensor("s_" + name, shape, dt, kind="Internal").ap()
    io.q_hi, io.q_lo = scratch("q_hi", [W_SB, S]), scratch("q_lo", [W_SB, S])
    io.k_hi, io.k_lo = scratch("k_hi", [W_SB, S]), scratch("k_lo", [W_SB, S])
    io.dv = scratch("dv", [S, W_SB])
    io.mix_t = scratch("mix_t", [D, S])
    io.h = scratch("h", [S, D])
    io.u2 = scratch("u2", [S, D])
    io.ys = scratch("ys", [MAX_TILES * P, D])
    with ExitStack() as ctx:
        sb, ps, sem = alloc(nc, ctx)
        k = Names()
        k.passed = sem("passed")
        k.spare_filled = sem("spare_filled")
        k.x_gathered = sem("x_gathered")
        k.y_gathered = [sem(f"y_gathered{i}") for i in range(4)]
        k.ident, k.ident_r, k.ident_bf = sb("ident", [P, P]), sb("ident_r", [P, P], F32R), sb("ident_bf", [P, P], BF16)
        k.before, k.ones_bf, k.ones = sb("before", [P, P], BF16), sb("ones_bf", [P, P], BF16), sb("ones", [P, 1])
        k.mask = sb("mask", [P, P], BF16)
        k.g_norm1, k.g_mix = sb("g_norm1", [P, DC]), sb("g_mix", [P, DC])
        k.conv_b, k.conv_w = sb("conv_b", [P, NL]), sb("conv_w", [P, CONV, NL])
        k.b_r, k.b_i, k.lam = sb("b_r", [P, NL]), sb("b_i", [P, NL]), sb("lam", [P, NL])
        k.b_router = sb("b_router", [P, NGRP + NE])
        k.v_last = sb("v_last", [P, NP * NT])
        k.eps = sb("eps", [P, 1])
        constants(nc, k, io)
        for stage in (qkv, lru, attention):
            stage(nc, k, io)
        k.logits = sb("logits", [P, NT * (NGRP + NE)])
        k.weight = sb("weight", [P, TOPK, NT])
        k.slot = sb("slot", [P, TOPK, NT], I32)
        k.tile_expert, k.tile_last = sb("tile_expert", [1, WIDE], I32), sb("tile_last", [1, WIDE], I32)
        k.ids = sb("ids", [P, WIDE], I32)
        k.tile_count = sb("tile_count", [1, 1], I32)
        for stage in (mix, routed_experts, combine):
            stage(nc, k, io)


INPUTS = ["x", "norm1_g", "w_in", "conv_w", "conv_b", "w_rgate", "b_rgate", "w_igate", "b_igate", "lam",
          "sb_norm_g", "lru_norm_g", "w_out", "norm2_g", "w_group", "b_group", "w_fine", "b_fine",
          "w_e_gate", "w_e_up", "w_e_down", "final_g"]


def kernel(**inputs):
    import concourse.bacc as bacc
    from concourse.bass_utils import run_bass_kernel_spmd

    nc = bacc.Bacc("TRN2", target_bir_lowering=False, num_devices=1)
    io, arrays = Names(), {}
    batch = inputs["x"].shape[0]
    for name in INPUTS:
        a = np.ascontiguousarray(inputs[name])
        if name == "x":
            a = a.reshape(batch * S, D)
        arrays["in_" + name] = a
        ap = nc.dram_tensor("in_" + name, a.shape, mybir.dt.from_np(a.dtype), kind="ExternalInput").ap()
        io.__dict__[name] = ap
    io.out = nc.dram_tensor("out", (batch * S, D), F32, kind="ExternalOutput").ap()
    build(nc, io)
    result = run_bass_kernel_spmd(nc, [arrays], core_ids=[0])
    return result.results[0]["out"].reshape(batch, S, D)
```
